# Optimizing a Trainium2 kernel written in Bass

```python
import math
import jax, jax.numpy as jnp
from jax import lax
import numpy as np

D_MODEL = 1024
BATCH = 1
SEQ = 256
DEPTH = 2

N_HEADS = 8
QK_NOPE_DIM = 64
QK_ROPE_DIM = 32
V_HEAD_DIM = 64
Q_LORA_RANK = 384
KV_LORA_RANK = 256
ROPE_THETA = 10000.0
Q_BLOCK = 128
CONV_CHANNELS = 512
CONV_WIDTH = 31
POOL_WINDOWS = (2, 4, 8, 16)
POOL_GROUPS = 4
POOL_CHANNELS = 512
POOL_GROUP_DIM = POOL_CHANNELS // POOL_GROUPS
N_BRANCHES = 3
D_FF = -(-8 * D_MODEL // (3 * 256)) * 256
EPS = 1e-6
IN_WIDTHS = (Q_LORA_RANK, KV_LORA_RANK, QK_ROPE_DIM, 2 * CONV_CHANNELS, POOL_CHANNELS, N_BRANCHES * D_MODEL)
D_IN = sum(IN_WIDTHS)

kernel_name = "hybrid_mla_conformer_pool_gated_block"

def rms_norm(x, g):
    x32 = x.astype(jnp.float32)
    y = x32 * lax.rsqrt(jnp.mean(x32 * x32, axis=-1, keepdims=True) + EPS)
    return (y * g.astype(jnp.float32)).astype(x.dtype)

def layer_norm(x, g, b):
    x32 = x.astype(jnp.float32)
    mu = jnp.mean(x32, axis=-1, keepdims=True)
    xc = x32 - mu
    y = xc * lax.rsqrt(jnp.mean(xc * xc, axis=-1, keepdims=True) + EPS)
    return (y * g.astype(jnp.float32) + b.astype(jnp.float32)).astype(x.dtype)

def rope_tables(positions):
    inv_freq = ROPE_THETA ** (-jnp.arange(0, QK_ROPE_DIM, 2, dtype=jnp.float32) / QK_ROPE_DIM)
    ang = positions.astype(jnp.float32)[..., None] * inv_freq
    return jnp.cos(ang), jnp.sin(ang)

def apply_rope(x, cos, sin):
    x32 = x.astype(jnp.float32)
    half = x32.shape[-1] // 2
    x1, x2 = x32[..., :half], x32[..., half:]
    out = jnp.concatenate([x1 * cos - x2 * sin, x2 * cos + x1 * sin], axis=-1)
    return out.astype(x.dtype)

def mla_branch(c_q, c_kv, k_rope_raw, cos, sin, q_norm, w_uq, kv_norm, w_uk, w_uv, w_o):
    B, S, _ = c_q.shape
    q = (rms_norm(c_q, q_norm) @ w_uq).reshape(B, S, N_HEADS, QK_NOPE_DIM + QK_ROPE_DIM)
    q_nope = q[..., :QK_NOPE_DIM]
    q_rope = apply_rope(q[..., QK_NOPE_DIM:], cos[:, :, None, :], sin[:, :, None, :])
    c_kv_n = rms_norm(c_kv, kv_norm)
    k_nope = (c_kv_n @ w_uk).reshape(B, S, N_HEADS, QK_NOPE_DIM)
    v = (c_kv_n @ w_uv).reshape(B, S, N_HEADS, V_HEAD_DIM)
    k_rope = apply_rope(k_rope_raw, cos, sin)
    nb = S // Q_BLOCK
    qn_blocks = q_nope.reshape(B, nb, Q_BLOCK, N_HEADS, QK_NOPE_DIM).transpose(1, 0, 2, 3, 4)
    qr_blocks = q_rope.reshape(B, nb, Q_BLOCK, N_HEADS, QK_ROPE_DIM).transpose(1, 0, 2, 3, 4)
    starts = jnp.arange(nb, dtype=jnp.int32) * Q_BLOCK
    key_idx = jnp.arange(S, dtype=jnp.int32)
    scale = 1.0 / math.sqrt(QK_NOPE_DIM + QK_ROPE_DIM)

    def attend(args):
        qn, qr, start = args
        s = jnp.einsum('bqhd,bkhd->bhqk', qn, k_nope) + jnp.einsum('bqhr,bkr->bhqk', qr, k_rope)
        s = s.astype(jnp.float32) * scale
        q_idx = start + jnp.arange(Q_BLOCK, dtype=jnp.int32)
        causal = key_idx[None, :] <= q_idx[:, None]
        s = jnp.where(causal[None, None], s, -jnp.inf)
        p = jax.nn.softmax(s, axis=-1).astype(v.dtype)
        return jnp.einsum('bhqk,bkhd->bqhd', p, v)

    o = lax.map(attend, (qn_blocks, qr_blocks, starts))
    o = o.transpose(1, 0, 2, 3, 4).reshape(B, S, N_HEADS * V_HEAD_DIM)
    return o @ w_o

def conv_branch(u, conv_w, conv_b, ln_g, ln_b, w_out):
    a, g = jnp.split(u, 2, axis=-1)
    h = a * jax.nn.sigmoid(g)
    h = lax.conv_general_dilated(h, conv_w[:, None, :], window_strides=(1,),
                                 padding=[(CONV_WIDTH - 1, 0)],
                                 dimension_numbers=('NWC', 'WIO', 'NWC'),
                                 feature_group_count=CONV_CHANNELS) + conv_b
    h = jax.nn.silu(layer_norm(h, ln_g, ln_b))
    return h @ w_out

def pool_branch(u, pool_w, pool_scale, w_out):
    B, S, _ = u.shape
    u32 = u.astype(jnp.float32).reshape(B, S, POOL_GROUPS, POOL_GROUP_DIM)
    cs = jnp.cumsum(u32, axis=1)
    t = jnp.arange(S, dtype=jnp.int32)
    outs = []
    for gi, w in enumerate(POOL_WINDOWS):
        c = cs[:, :, gi]
        lag = jnp.pad(c, ((0, 0), (w, 0), (0, 0)))[:, :S]
        count = jnp.minimum(t + 1, w).astype(jnp.float32)[None, :, None]
        outs.append((c - lag) / count)
    pooled = jnp.stack(outs, axis=2)
    d = (pooled - u32).astype(u.dtype)
    m = jnp.einsum('bsgc,gcd->bsgd', d, pool_w).reshape(B, S, POOL_CHANNELS) * pool_scale
    return m @ w_out

def mixer_sublayer(x, cos, sin, norm_pre, w_in, q_norm, w_uq, kv_norm, w_uk, w_uv, w_attn_o,
                   conv_w, conv_b, conv_ln_g, conv_ln_b, w_conv_o, pool_w, pool_scale, w_pool_o,
                   w_mix_o, norm_post):
    B, S, D = x.shape
    h = rms_norm(x, norm_pre)
    z = h @ w_in
    split_at = [int(v) for v in np.cumsum(IN_WIDTHS)[:-1]]
    c_q, c_kv, k_r, u_conv, u_pool, gate_logits = jnp.split(z, split_at, axis=-1)
    y_attn = mla_branch(c_q, c_kv, k_r, cos, sin, q_norm, w_uq, kv_norm, w_uk, w_uv, w_attn_o)
    y_conv = conv_branch(u_conv, conv_w, conv_b, conv_ln_g, conv_ln_b, w_conv_o)
    y_pool = pool_branch(u_pool, pool_w, pool_scale, w_pool_o)
    gates = jax.nn.sigmoid(gate_logits.astype(jnp.float32)).astype(x.dtype).reshape(B, S, N_BRANCHES, D)
    merged = gates[:, :, 0] * y_attn + gates[:, :, 1] * y_conv + gates[:, :, 2] * y_pool
    return rms_norm(merged @ w_mix_o, norm_post)

def ffn_sublayer(x, norm_pre, w_gate, w_up, w_down, norm_post):
    h = rms_norm(x, norm_pre)
    y = (jax.nn.silu(h @ w_gate) * (h @ w_up)) @ w_down
    return rms_norm(y, norm_post)

def setup_inputs(seed: int = 0) -> dict:
    key = jax.random.key(seed)
    ks = jax.random.split(key, 32)
    L, D = DEPTH, D_MODEL

    def dense(k, shape, fan_in):
        return jax.random.normal(k, shape, jnp.float32) * fan_in ** -0.5

    def gain(k, shape):
        return 1.0 + 0.02 * jax.random.normal(k, shape, jnp.float32)

    x = jax.random.normal(ks[0], (BATCH, SEQ, D), jnp.float32)
    offsets = jax.random.randint(ks[1], (BATCH, 1), 0, 4096, dtype=jnp.int32)
    positions = offsets + jnp.arange(SEQ, dtype=jnp.int32)[None, :]
    return {
        "x": x,
        "positions": positions,
        "mix_norm_pre": gain(ks[2], (L, D)),
        "w_in": dense(ks[3], (L, D, D_IN), D),
        "q_norm": gain(ks[4], (L, Q_LORA_RANK)),
        "w_uq": dense(ks[5], (L, Q_LORA_RANK, N_HEADS * (QK_NOPE_DIM + QK_ROPE_DIM)), Q_LORA_RANK),
        "kv_norm": gain(ks[6], (L, KV_LORA_RANK)),
        "w_uk": dense(ks[7], (L, KV_LORA_RANK, N_HEADS * QK_NOPE_DIM), KV_LORA_RANK),
        "w_uv": dense(ks[8], (L, KV_LORA_RANK, N_HEADS * V_HEAD_DIM), KV_LORA_RANK),
        "w_attn_o": dense(ks[9], (L, N_HEADS * V_HEAD_DIM, D), N_HEADS * V_HEAD_DIM),
        "conv_w": dense(ks[10], (L, CONV_WIDTH, CONV_CHANNELS), CONV_WIDTH),
        "conv_b": 0.02 * jax.random.normal(ks[11], (L, CONV_CHANNELS), jnp.float32),
        "conv_ln_g": gain(ks[12], (L, CONV_CHANNELS)),
        "conv_ln_b": 0.02 * jax.random.normal(ks[13], (L, CONV_CHANNELS), jnp.float32),
        "w_conv_o": dense(ks[14], (L, CONV_CHANNELS, D), CONV_CHANNELS),
        "pool_w": dense(ks[15], (L, POOL_GROUPS, POOL_GROUP_DIM, POOL_GROUP_DIM), POOL_GROUP_DIM),
        "pool_scale": 1.0 + 0.1 * jax.random.normal(ks[16], (L, POOL_CHANNELS), jnp.float32),
        "w_pool_o": dense(ks[17], (L, POOL_CHANNELS, D), POOL_CHANNELS),
        "w_mix_o": dense(ks[18], (L, D, D), D),
        "mix_norm_post": gain(ks[19], (L, D)),
        "ffn_norm_pre": gain(ks[20], (L, D)),
        "w_gate": dense(ks[21], (L, D, D_FF), D),
        "w_up": dense(ks[22], (L, D, D_FF), D),
        "w_down": dense(ks[23], (L, D_FF, D), D_FF),
        "ffn_norm_post": gain(ks[24], (L, D)),
    }

def reference(x, positions, mix_norm_pre, w_in, q_norm, w_uq, kv_norm, w_uk, w_uv, w_attn_o,
              conv_w, conv_b, conv_ln_g, conv_ln_b, w_conv_o, pool_w, pool_scale, w_pool_o,
              w_mix_o, mix_norm_post, ffn_norm_pre, w_gate, w_up, w_down, ffn_norm_post):
    cos, sin = rope_tables(positions)
    h = x
    for l in range(DEPTH):
        h = h + mixer_sublayer(h, cos, sin, mix_norm_pre[l], w_in[l], q_norm[l], w_uq[l], kv_norm[l],
                               w_uk[l], w_uv[l], w_attn_o[l], conv_w[l], conv_b[l], conv_ln_g[l],
                               conv_ln_b[l], w_conv_o[l], pool_w[l], pool_scale[l], w_pool_o[l],
                               w_mix_o[l], mix_norm_post[l])
        h = h + ffn_sublayer(h, ffn_norm_pre[l], w_gate[l], w_up[l], w_down[l], ffn_norm_post[l])
    return h


_drawn_inputs = setup_inputs


def setup_inputs(seed=0):
    import zlib

    import numpy as np

    out = dict(_drawn_inputs(seed))
    spreads = {}
    factors = {'q_norm': 8.0,
     'kv_norm': 8.0,
     'conv_ln_g': 12.088,
     'conv_ln_b': 21.094,
     'ffn_norm_post': 3.576,
     'pool_scale': 3.719}
    for name, (base, spread) in spreads.items():
        noise = np.random.default_rng([zlib.crc32(name.encode()), seed]).standard_normal(out[name].shape)
        drawn = base * np.exp(spread * noise) if base else spread * noise
        out[name] = __import__('jax').numpy.asarray(drawn.astype(out[name].dtype))
    for name, factor in factors.items():
        out[name] = (out[name] * factor).astype(out[name].dtype)
    return out
```

```python
from contextlib import ExitStack

import concourse.bass as bass
import numpy as np
from concourse import mybir

F32 = mybir.dt.float32
F32R = mybir.dt.float32r
I32 = mybir.dt.int32
ALU = mybir.AluOpType
ACT = mybir.ActivationFunctionType
AX_X = mybir.AxisListType.X

P = 128
LAYERS, SEQ, D = 2, 256, 1024
TOK = SEQ // P
KD = D // P
HEADS, NOPE, ROPE, VDIM = 8, 64, 32, 64
QK = NOPE + ROPE
HR = ROPE // 2
Q_RANK, KV_RANK = 384, 256
CONV, TAPS = 512, 31
CT = CONV // P
POOL_WINDOWS = (2, 4, 8, 16)
D_FF = 2816
FT = D_FF // P
EPS = 1e-6
SCALE = float(1.0 / np.sqrt(QK))
MASKED = -3.0e38
TWO_PI = 6.283185307179586
PI_BELOW = 3.1415925
ROUND = 12582912.0
TURN = (6.28125, 0.0019350051879882812, 3.01991598196e-07)

WU = 1024
RING = 4
(U_G, U_A, U_CQ, U_CKV, U_POOL, U_Q, U_K, U_V, U_MT, U_GATE, U_POOLO, U_CONVO, U_ATTNO, U_MIX, U_FFN,
 U_LAST, U_DOWN, UNITS) = (0, 4, 8, 12, 16, 20, 23, 24, 25, 26, 50, 54, 58, 62, 70, 110, 114, 136)
CKV_W = KV_RANK + ROPE
FULL_CHUNKS = 5
LAST_W = D_FF - 512 * FULL_CHUNKS

A_G, A_CQ, A_POOL, A_K = 0, 1, 2, 3
B_A, B_CKV, B_Q, B_V = 0, 1, 2, 3
ACC_GATE, ACC_POOLO, ACC_CONVO, ACC_ATTNO, ACC_MIX, ACC_FFN, ACC_LAST, ACC_DOWN, ACC_USES = (
    4, 7, 8, 9, 10, 11, 16, 17, 18)
T_X, T_HC, T_CQ, T_CKV, T_Q, T_MT, T_K, T_P, T_O, T_M, T_F, T_H, T_HLAST, T_USES = (
    0, 4, 6, 8, 10, 14, 16, 20, 28, 30, 34, 38, 48, 50)
M_Q, M_D, M_MEAN, M_VAR, M_S, M_USES = 0, 2, 4, 5, 6, 14
R_X, R_CQ, R_CKV, R_MIX, R_F, R_DOWN, NSTAT = 0, 2, 4, 6, 8, 10, 12
STAT_WIDTH = [D, D, Q_RANK, Q_RANK, KV_RANK, KV_RANK, D, D, D, D, D, D]
C_PRE, C_PREF, C_QN, C_KVN, C_PS, C_CB, C_LG, C_LB, C_CW, NPAR = 0, 8, 16, 19, 21, 25, 29, 33, 37, 161
K_ID, K_FREQ, K_ONE, K_MASK, K_BAND, NCONST = 0, 128, 144, 272, 400, 1936
BANDW = SEQ + P
H_CKV, H_CQ, H_O, H_CONV, H_POOL, H_Q = 3, 0, 0, 5, 9, 13
STEPS = HEADS // 2 * TOK
SHARE = 5
OWN = TAPS - SHARE
DVE_STEPS = 110


LAST_UNIT = (
    {A_G: 3, A_CQ: 11, A_POOL: 19, A_K: 23, ACC_GATE: 29, ACC_POOLO: 51, ACC_CONVO: 55, ACC_ATTNO: 59,
     ACC_FFN: 73, ACC_FFN + 1: 81, ACC_LAST: 111},
    {B_A: 7, B_CKV: 15, B_Q: 22, B_V: 24, ACC_GATE: 33, ACC_POOLO: 53, ACC_CONVO: 57, ACC_ATTNO: 61,
     ACC_FFN: 77, ACC_FFN + 1: 85, ACC_LAST: 113})
FULL_COUNT = (16, 15)


def full_count(pair, use):
    return use + 1 - (use > ACC_MIX) - (pair == 1 and use > B_Q)


MISC_FULL = (3, 2)
TP_FULL = (T_USES // 2, T_USES // 2 - 1)


def tp_count(n):
    return n // 2 + 1 - (n % 2 == 1 and n > T_MT + 1)


def hi_count(n):
    return n + 1 if n < T_HC else n - 1 if n < T_P else n - 9


def mul_count(n):
    return n + 1 if n < 4 else n - 1 if n < 10 else n - 5 if n < 16 else n - 23


def build(nc, W, par_d, const_d, gain_d, x_d, pos_d, out_d):
    with ExitStack() as ctx:
        def sb(name, shape, dt=F32):
            return ctx.enter_context(nc.sbuf_tensor(name, shape, dt))

        def sem(name):
            return ctx.enter_context(nc.semaphore(name))

        raw = sb("raw", [P, RING, WU])
        w_hi = sb("w_hi", [P, RING, WU], F32R)
        w_lo = sb("w_lo", [P, RING, WU], F32R)
        x = sb("x_sb", [P, TOK, D])
        xT_hi = sb("xT_hi", [P, KD, SEQ], F32R)
        xT_lo = sb("xT_lo", [P, KD, SEQ], F32R)
        hT_hi = sb("hT_hi", [P, FT, SEQ], F32R)
        hT_lo = sb("hT_lo", [P, FT, SEQ], F32R)
        gain = sb("gain", [P, D])
        const = sb("const", [P, NCONST])
        par2 = sb("par2", [P, LAYERS, NPAR])
        par = sb("par", [P, NPAR])
        cq = sb("cq", [P, TOK, Q_RANK + CKV_W])
        hc = sb("hc", [P, TOK, CONV])
        sg = sb("sg", [P, TOK, 512])
        u_sb = sb("u_sb", [P, TOK, 512])
        hcT = sb("hcT", [P, CT, TAPS - 1 + SEQ])
        cacc = sb("cacc", [P, CT, SEQ])
        cacc_odd = sb("cacc_odd", [P, SEQ])
        cprod = sb("cprod", [P, SEQ])
        gates = sb("gates", [P, TOK, 3 * D])
        qk = sb("qk", [P, 2, TOK, HEADS * QK])
        v_sb = sb("v_sb", [P, TOK, HEADS * VDIM])
        tmp = sb("tmp", [P, 2, 512])
        rope_a = sb("rope_a", [P, 256])
        rope_b = sb("rope_b", [P, 256])
        cos2 = sb("cos2", [P, TOK, ROPE])
        sin2 = sb("sin2", [P, TOK, ROPE])
        ang = sb("ang", [P, 6, TOK, HR])
        pos_i = sb("pos_i", [P, TOK], I32)
        pos_f = sb("pos_f", [P, TOK])
        ssq = sb("ssq", [P, NSTAT])
        mean2 = sb("mean2", [P, NSTAT])
        rstd = sb("rstd", [P, NSTAT])
        cvar = sb("cvar", [P, TOK])
        crstd = sb("crstd", [P, TOK])
        half = sb("half", [P, 1])
        mx = sb("mx", [P, 2, 2])
        nmx = sb("nmx", [P, 2, 2])
        rsum = sb("rsum", [P, 2, 2])
        rinv = sb("rinv", [P, 2, 2])

        q_sb, k_sb = qk[:, 0], qk[:, 1]
        qk_flat = qk[:, :, :, :].rearrange("p a t n -> p (a t n)")
        probs = qk_flat[:, 0:1024].rearrange("p (b i n) -> p b i n", b=2, i=2)
        pT = qk_flat[:, 1024:2048].rearrange("p (b i n) -> p b i n", b=2, i=4)
        o_sb = qk_flat[:, 2048:3072].rearrange("p (t n) -> p t n", t=TOK)
        junk = qk_flat[:, 0:D]
        xc = hc[:, :, :].rearrange("p t n -> p (t n)").rearrange("p (c n) -> p c n", c=CT)
        sq = sg[:, :, :].rearrange("p t n -> p (t n)").rearrange("p (c n) -> p c n", c=CT)
        hid = u_sb
        ident = const[:, K_ID:K_ID + P]
        ones = const[:, K_ONE:K_ONE + P]
        mask = const[:, K_MASK:K_MASK + P]

        acc = ctx.enter_context(nc.psum_tensor("acc", [P, 4, 512], F32))
        tp = ctx.enter_context(nc.psum_tensor("tp", [P, 2, 512], F32))
        misc = ctx.enter_context(nc.psum_tensor("misc", [P, 2, 512], F32))

        raw_in = [sem(f"raw_in{s}") for s in range(RING)]
        hi_done = sem("hi_done")
        lo_done = sem("lo_done")
        unit_used = sem("unit_used")
        full = [sem(f"full{b}") for b in range(2)]
        wide_full = sem("wide_full")
        free = [sem(f"free{b}") for b in range(4)]
        tp_full = [sem(f"tp_full{b}") for b in range(2)]
        tp_free = [sem(f"tp_free{b}") for b in range(2)]
        tp_hi = sem("tp_hi")
        mul_done = sem("mul_done")
        misc_full = [sem(f"misc_full{b}") for b in range(2)]
        misc_free = [sem(f"misc_free{b}") for b in range(2)]
        d_hi = sem("d_hi")
        const_in = sem("const_in")
        band_in = sem("band_in")
        x_in = [sem(f"x_in{t}") for t in range(TOK)]
        setup = sem("setup")
        ang_ready = sem("ang_ready")
        tables = sem("tables")
        par_ready = sem("par_ready")
        x_ready = [sem(f"x_ready{t}") for t in range(TOK)]
        ssq_done = sem("ssq_done")
        r_done = sem("r_done")
        mean_done = sem("mean_done")
        gain_in = sem("gain_in")
        gain_used = sem("gain_used")
        pad_zero = sem("pad_zero")
        q_roped = sem("q_roped")
        k_roped = sem("k_roped")
        k_nope = sem("k_nope")
        conv_dve = sem("conv_dve")
        pool_step = sem("pool_step")
        pool_went = sem("pool_went")
        conv_pool = sem("conv_pool")
        centred = sem("centred")
        sq_done = sem("sq_done")
        var_in = sem("var_in")
        cstd = sem("cstd")
        diag_done = sem("diag_done")
        spread = sem("spread")
        csilu = sem("csilu")
        conv_hi = sem("conv_hi")
        conv_lo = sem("conv_lo")
        s_done = sem("s_done")
        nm_done = sem("nm_done")
        exp_done = sem("exp_done")
        pv_done = sem("pv_done")
        gated = sem("gated")
        summed = sem("summed")
        merged = sem("merged")
        dve_step = sem("dve_step")
        stored = sem("stored")

        block = ctx.enter_context(nc.Block())

        @block.sync
        def _(sp):
            def load_x(t):
                sp.dma_start(x[:, t, :], x_d[t * P:(t + 1) * P, :]).then_inc(x_in[t], 16)

            load_x(0)
            sp.dma_start(const[:, 0:K_BAND], const_d[:, 0:K_BAND]).then_inc(const_in, 16)
            sp.dma_start(par2[:, :, :], par_d).then_inc(const_in, 16)
            sp.dma_start(pos_i[:, :], pos_d).then_inc(const_in, 16)
            load_x(1)

            with sp.Fori(0, LAYERS) as l:
                def load(u, s, width):
                    sp.wait_ge(lo_done, l * UNITS + u + 1)
                    sp.dma_start(raw[:, s, 0:width],
                                 W[bass.ds((l * UNITS + u) * P, P), 0:width]).then_inc(raw_in[s], 16)

                def loads(first, last, width):
                    if last - first < 2 * RING:
                        for u in range(first, last):
                            load(u, u % RING, width)
                        return
                    with sp.Fori(0, (last - first) // RING) as i:
                        for s in range(RING):
                            load(i * RING + (first + s), (first + s) % RING, width)
                    for u in range(first + (last - first) // RING * RING, last):
                        load(u, u % RING, width)

                def load_gain(n):
                    sp.wait_ge(gain_used, l * 4 + 2 * n + 1)
                    sp.dma_start(gain[:, :], gain_d[bass.ds(l * 2 + n, 1), :].to_broadcast((P, D))
                                 ).then_inc(gain_in, 16)

                loads(U_G, U_CQ, 1024)
                load_gain(0)
                loads(U_CQ, U_CKV, 2 * Q_RANK)
                loads(U_CKV, U_POOL, 2 * CKV_W)
                loads(U_POOL, U_Q, 1024)
                loads(U_Q, U_K, HEADS * QK)
                loads(U_K, U_MT, 1024)
                loads(U_MT, U_GATE, 512)
                loads(U_GATE, U_FFN + 12, 1024)
                load_gain(1)
                loads(U_FFN + 12, UNITS, 1024)

            for t in range(TOK):
                sp.wait_ge(x_ready[t], 4 * LAYERS + 2)
                sp.dma_start(out_d[t * P:(t + 1) * P, :], x[:, t, :]).then_inc(stored, 16)
            sp.wait_ge(stored, 16 * TOK)

        @block.tensor
        def _(pe):
            pe.sem_inc(unit_used, RING)
            for b in range(4):
                pe.sem_inc(free[b], 1)
            for b in range(2):
                pe.sem_inc(tp_free[b], 1)
                pe.sem_inc(misc_free[b], 1)
            pe.wait_ge(const_in, 48)

            with pe.Fori(0, LAYERS) as l:
                def mm3(out, a_hi, a_lo, b_hi, b_lo, start, stop):
                    pe.matmul(out, a_hi, b_hi, start=start, stop=False)
                    pe.matmul(out, a_hi, b_lo, start=False, stop=False)
                    return pe.matmul(out, a_lo, b_hi, start=False, stop=stop)

                def unit_ready(u, off=0):
                    pe.wait_ge(lo_done, l * UNITS + off + (RING + u + 1))

                def bank_free(b, use, off=0):
                    pe.wait_ge(free[b], l * ACC_USES + off + (use + 1))

                def tok_mm(u, t, kts, width, banks, srcT, first, last):
                    s_hi, s_lo = srcT
                    s = u % RING
                    for i, kt in enumerate(kts):
                        for g, b in enumerate(banks):
                            c = (i * len(banks) + g) * width
                            mm = mm3(b, s_hi[:, kt, t * P:(t + 1) * P], s_lo[:, kt, t * P:(t + 1) * P],
                                     w_hi[:, s, c:c + width], w_lo[:, s, c:c + width],
                                     kt == first, kt == last)
                    return mm

                XT, HT = (xT_hi, xT_lo), (hT_hi, hT_lo)

                def col_group(u0, n, per, width, pair, use, srcT, kt0=0, uoff=0, aoff=0):
                    for i in range(n):
                        unit_ready(u0 + i, uoff)
                        for t in range(TOK):
                            b = 2 * pair + t
                            if i == 0:
                                bank_free(b, use, aoff)
                            kts = [kt0 + i * per + k for k in range(per)]
                            mm = tok_mm(u0 + i, t, kts, width, [acc[:, b, 0:width]], srcT,
                                        kt0, kt0 + n * per - 1)
                            if t == 1:
                                mm.then_inc(unit_used, 1)
                            elif i == n - 1:
                                mm.then_inc(full[pair], 1)

                def transposes(n, blocks, off=0):
                    b = n % 2
                    pe.wait_ge(tp_free[b], l * (T_USES // 2) + off + (n // 2 + 1))
                    for i, (src, rows) in enumerate(blocks):
                        mm = pe.transpose(tp[0:rows, b, i * P:(i + 1) * P], src, ident)
                    mm.then_inc(tp_full[b], 1)

                def stored_T(n, off=0):
                    pe.wait_ge(tp_free[n % 2], l * (T_USES // 2) + off + (n // 2 + 2))

                def x_transposes(n0, t, ready):
                    for h in range(2):
                        pe.wait_ge(x_ready[t], l * 4 + (2 * ready - 1 + h))
                        transposes(n0 + 2 * t + h,
                                   [(x[:, t, (4 * h + k) * P:(4 * h + k + 1) * P], P) for k in range(4)])

                def first_group(u0, n0, use, pair, ready):
                    for t in range(TOK):
                        stored_T(n0 + 2 * t)
                        stored_T(n0 + 2 * t + 1)
                        bank_free(2 * pair + t, use)
                        for i in range(4):
                            if t == 0:
                                if i == 3:
                                    x_transposes(n0, 1, ready)
                                unit_ready(u0 + i)
                            mm = tok_mm(u0 + i, t, [2 * i, 2 * i + 1], 512,
                                        [acc[:, 2 * pair + t, :]], XT, 0, KD - 1)
                            if t == 1:
                                mm.then_inc(unit_used, 1)
                            elif i == 3:
                                mm.then_inc(full[pair], 1)

                def wide_group(u0, n, use, srcT, waits, ahead=None):
                    def one(i, t):
                        if i == 0:
                            bank_free(2 * t, use)
                            bank_free(2 * t + 1, use)
                        mm = tok_mm(u0 + i, t, [i], 512, [acc[:, 2 * t, :], acc[:, 2 * t + 1, :]],
                                    srcT, 0, n - 1)
                        if t == 1:
                            mm.then_inc(unit_used, 1)
                        elif i == n - 1:
                            mm.then_inc(wide_full, 1)

                    for i in range(n - 4):
                        waits(i)
                        unit_ready(u0 + i)
                        for t in range(TOK):
                            one(i, t)
                    for t in range(TOK):
                        for i in range(n - 4, n):
                            if t == 0:
                                waits(i)
                                unit_ready(u0 + i)
                            elif i == n - 1 and ahead:
                                ahead()
                            one(i, t)

                x_transposes(T_X, 0, 1)
                first_group(U_G, T_X, A_G, 0, 1)
                col_group(U_A, 4, 2, 512, 1, B_A, XT)
                col_group(U_CQ, 4, 2, Q_RANK, 0, A_CQ, XT)
                for t in range(TOK):
                    pe.wait_ge(free[2 + t], l * ACC_USES + (B_A + 2))
                    transposes(T_HC + t, [(hc[:, t, c * P:(c + 1) * P], P) for c in range(CT)])
                col_group(U_CKV, 4, 2, CKV_W, 1, B_CKV, XT)
                for t in range(TOK):
                    pe.wait_ge(free[t], l * ACC_USES + (A_CQ + 2))
                    transposes(T_CQ + t, [(cq[:, t, c * P:(c + 1) * P], P) for c in range(3)])
                col_group(U_POOL, 4, 2, 512, 0, A_POOL, XT)
                for t in range(TOK):
                    pe.wait_ge(free[2 + t], l * ACC_USES + (B_CKV + 2))
                    transposes(T_CKV + t, [(cq[:, t, c * P:(c + 1) * P], P) for c in range(3, 5)])
                for i in range(3):
                    unit_ready(U_Q + i)
                    for t in range(TOK):
                        if i == 0:
                            stored_T(T_CQ + t)
                            bank_free(2 + t, B_Q)
                            pe.wait_ge(misc_free[t], l * (M_USES // 2) + 1)
                        mm = tok_mm(U_Q + i, t, [i], 384, [acc[:, 2 + t, 0:384], misc[:, t, 0:384]], HT, 0, 2)
                        if t == 1:
                            mm.then_inc(unit_used, 1)
                        elif i == 2:
                            mm.then_inc(misc_full[0], 1)
                for t in range(TOK):
                    stored_T(T_CKV + t)
                col_group(U_K, 1, 2, 512, 0, A_K, HT, kt0=H_CKV)
                col_group(U_V, 1, 2, 512, 1, B_V, HT, kt0=H_CKV)
                for t in range(TOK):
                    pe.wait_ge(free[t], l * ACC_USES + (A_POOL + 2))
                pe.wait_ge(band_in, 16)
                for h in range(2):
                    pe.wait_ge(misc_free[h], l * (M_USES // 2) + (M_D // 2 + 1))
                    for g in range(2 * h, 2 * h + 2):
                        band = const[:, K_BAND + g * BANDW:K_BAND + (g + 1) * BANDW]
                        c = (g % 2) * SEQ
                        pe.matmul(misc[:, h, c:c + SEQ], u_sb[:, 0, g * P:(g + 1) * P], band[:, 0:SEQ],
                                  start=True, stop=False)
                        mm = pe.matmul(misc[:, h, c + P:c + SEQ], u_sb[:, 1, g * P:(g + 1) * P],
                                       band[:, SEQ:BANDW], start=False, stop=True)
                    mm.then_inc(misc_full[h], 1)
                for n in range(4):
                    hh, t = n // 2, n % 2
                    if hh == 0:
                        pe.wait_ge(q_roped, l * TOK + (t + 1))
                    transposes(T_Q + n, [(q_sb[:, t, h * QK:(h + 1) * QK], QK) for h in range(4 * hh, 4 * hh + 4)])
                unit_ready(U_MT)
                for h in range(2):
                    pe.wait_ge(misc_free[h], l * (M_USES // 2) + (M_D // 2 + 2))
                    b = (T_MT + h) % 2
                    pe.wait_ge(tp_free[b], l * (T_USES // 2) + ((T_MT + h) // 2 + 1))
                    for g in range(2 * h, 2 * h + 2):
                        s = U_MT % RING
                        mm = mm3(tp[:, b, (g % 2) * SEQ:(g % 2 + 1) * SEQ],
                                 w_hi[:, s, g * P:(g + 1) * P], w_lo[:, s, g * P:(g + 1) * P],
                                 hT_hi[:, H_CONV + g, :], hT_lo[:, H_CONV + g, :], True, True)
                    mm.then_inc(tp_full[b] if h == 0 else unit_used, 1)
                with pe.Fori(0, 3) as j:
                    for g in range(2):
                        for i in range(4):
                            u = U_GATE + 4 * g + i
                            pe.wait_ge(lo_done, l * UNITS + j * 8 + (RING + u + 1))
                            for t in range(TOK):
                                b = 2 * g + t
                                if i == 0:
                                    pe.wait_ge(free[b], l * ACC_USES + j + (ACC_GATE + 1))
                                mm = tok_mm(u, t, [2 * i, 2 * i + 1], 512, [acc[:, b, :]], XT, 0, KD - 1)
                                if t == 1:
                                    mm.then_inc(unit_used, 1)
                                elif i == 3:
                                    mm.then_inc(full[g], 1)
                for n in range(4):
                    hh, t = n // 2, n % 2
                    if hh == 0:
                        pe.wait_ge(k_roped, l * TOK + (t + 1))
                        pe.wait_ge(k_nope, l * TOK + (t + 1))
                    transposes(T_K + n, [(k_sb[:, t, h * QK:(h + 1) * QK], QK) for h in range(4 * hh, 4 * hh + 4)])
                pe.wait_ge(conv_dve, l * 3 + 3)
                pe.wait_ge(conv_pool, l * CT + CT)
                pe.wait_ge(misc_free[0], l * (M_USES // 2) + (M_MEAN // 2 + 1))
                for c in range(CT):
                    mm = pe.matmul(misc[:, 0, 0:SEQ], ones, cacc[:, c, :], start=c == 0, stop=c == CT - 1)
                mm.then_inc(misc_full[0], 1)

                def out_unit(u, halves=(0, 1)):
                    use = ACC_POOLO + (u - U_POOLO) // 4
                    src = (H_POOL, H_CONV, H_O)[(u - U_POOLO) // 4]
                    i, pair = (u - U_POOLO) % 2, (u - U_POOLO) % 4 // 2
                    for t in halves:
                        if t == 0:
                            unit_ready(u)
                        b = 2 * pair + t
                        if i == 0:
                            bank_free(b, use)
                        mm = tok_mm(u, t, [src + 2 * i, src + 2 * i + 1], 512, [acc[:, b, :]], HT, src, src + 3)
                        if t == 1:
                            mm.then_inc(unit_used, 1)
                        elif i == 1:
                            mm.then_inc(full[pair], 1)

                for h in range(2):
                    stored_T(T_MT + h)
                out_unit(U_POOLO)
                pe.wait_ge(sq_done, l + 1)
                pe.wait_ge(misc_free[1], l * (M_USES // 2) + (M_VAR // 2 + 1))
                for t in range(TOK):
                    for c in range(CT):
                        mm = pe.matmul(misc[:, 1, t:t + 1], sq[:, c, t * P:(t + 1) * P], ones[:, 0:1],
                                       start=c == 0, stop=c == CT - 1)
                mm.then_inc(misc_full[1], 1)

                def scores(n):
                    hp, t = n // 2, n % 2
                    keys = (t + 1) * P
                    if n == 0 or n == 4:
                        for k in range(2):
                            stored_T(T_K + n // 2 + k)
                    pe.wait_ge(misc_free[n % 2], l * (M_USES // 2) + ((M_S + n) // 2 + 1))
                    for i in range(2):
                        h = 2 * hp + i
                        q = slice(t * P, (t + 1) * P)
                        mm = mm3(misc[:, n % 2, i * keys:(i + 1) * keys],
                                 hT_hi[0:QK, H_Q + h, q], hT_lo[0:QK, H_Q + h, q],
                                 xT_hi[0:QK, h, 0:keys], xT_lo[0:QK, h, 0:keys], True, True)
                    mm.then_inc(s_done, 1)

                def p_transposes(n):
                    t = n % 2
                    pe.wait_ge(exp_done, l * STEPS + (n + 1))
                    transposes(T_P + n, [(probs[:, n % 2, i, k * P:(k + 1) * P], P)
                                         for i in range(2) for k in range(t + 1)])

                def weighted_values(n):
                    hp, t = n // 2, n % 2
                    stored_T(T_P + n)
                    for i in range(2):
                        h = 2 * hp + i
                        for k in range(t + 1):
                            mm = pe.matmul(misc[:, n % 2, i * VDIM:(i + 1) * VDIM],
                                           pT[:, n % 2, i * (t + 1) + k, :],
                                           v_sb[:, k, h * VDIM:(h + 1) * VDIM], start=k == 0, stop=k == t)
                    mm.then_inc(pv_done, 1)

                for n in range(STEPS + 2):
                    u = {**{k: U_POOLO + k for k in range(1, 7)}, 9: U_POOLO + 7}.get(n)
                    if u == U_CONVO:
                        pe.wait_ge(conv_lo, l + 1)
                    if n == 1:
                        pe.wait_ge(diag_done, l * TOK + TOK)
                        pe.matmul(misc[:, 1, 0:SEQ], ones, rope_a[:, :], start=True, stop=True
                                  ).then_inc(spread, 1)
                    if u:
                        out_unit(u, (0,))
                    if n >= 2:
                        weighted_values(n - 2)
                    if u:
                        out_unit(u, (1,))
                    if n < STEPS:
                        scores(n)
                    if 1 <= n <= STEPS:
                        p_transposes(n - 1)
                for t in range(TOK):
                    pe.wait_ge(misc_free[t], l * (M_USES // 2) + ((M_S + 6 + t) // 2 + 2))
                    transposes(T_O + t, [(o_sb[:, t, c * P:(c + 1) * P], P) for c in range(4)])
                for t in range(TOK):
                    stored_T(T_O + t)
                for u in range(U_ATTNO, U_ATTNO + 3):
                    out_unit(u)

                def merged_transposes(h):
                    for t in range(TOK):
                        pe.wait_ge(merged, l * 4 + (2 * h + t + 1))
                        transposes(T_M + 2 * h + t, [(gates[:, t, (4 * h + k) * P:(4 * h + k + 1) * P], P)
                                                     for k in range(4)])

                merged_transposes(0)
                out_unit(U_ATTNO + 3)

                def mix_waits(i):
                    if i == 2:
                        merged_transposes(1)
                    if i % 4 == 0:
                        stored_T(T_M + i // 2)
                        stored_T(T_M + i // 2 + 1)

                wide_group(U_MIX, KD, ACC_MIX, XT, mix_waits, lambda: x_transposes(T_F, 0, 2))

                first_group(U_FFN, T_F, ACC_FFN, 0, 2)
                col_group(U_FFN + 4, 4, 2, 512, 1, ACC_FFN, XT)

                with pe.Fori(0, FULL_CHUNKS - 1) as j:
                    for g in range(2):
                        for i in range(4):
                            u = U_FFN + 8 + 4 * g + i
                            pe.wait_ge(lo_done, l * UNITS + j * 8 + (RING + u + 1))
                            for t in range(TOK):
                                b = 2 * g + t
                                if i == 0:
                                    pe.wait_ge(free[b], l * ACC_USES + j + (ACC_FFN + 2))
                                mm = tok_mm(u, t, [2 * i, 2 * i + 1], 512, [acc[:, b, :]], XT, 0, KD - 1)
                                if t == 1:
                                    mm.then_inc(unit_used, 1)
                                elif i == 3:
                                    mm.then_inc(full[g], 1)
                        if g == 0:
                            for t in range(TOK):
                                pe.wait_ge(free[2 + t], l * ACC_USES + j + (ACC_FFN + 2))
                                pe.wait_ge(tp_free[t], l * (T_USES // 2) + j + (T_H // 2 + 1))
                                for c in range(4):
                                    mm = pe.transpose(tp[:, t, c * P:(c + 1) * P],
                                                      hid[:, t, c * P:(c + 1) * P], ident)
                                mm.then_inc(tp_full[t], 1)
                col_group(U_LAST, 2, 4, LAST_W, 0, ACC_LAST, XT)
                for t in range(TOK):
                    pe.wait_ge(free[2 + t], l * ACC_USES + (ACC_LAST + 1))
                    transposes(T_HLAST - 2 + t, [(hid[:, t, c * P:(c + 1) * P], P) for c in range(4)])
                col_group(U_LAST + 2, 2, 4, LAST_W, 1, ACC_LAST, XT)

                def down_waits(i):
                    if i == 2:
                        for t in range(TOK):
                            pe.wait_ge(free[2 + t], l * ACC_USES + (ACC_LAST + 2))
                            transposes(T_HLAST + t, [(hid[:, t, c * P:(c + 1) * P], P) for c in range(2)])
                    if i % 4 == 0:
                        for t in range(TOK):
                            stored_T(T_H + i // 2 + t)

                wide_group(U_DOWN, FT, ACC_DOWN, HT, down_waits)

        @block.scalar
        def _(act):
            act.preload_act_table(ACT.Sigmoid)
            with act.Fori(0, LAYERS) as l:
                def hi(u, off=0, width=None, uses=0):
                    s = u % RING
                    width = width or unit_width(u)
                    act.wait_ge(raw_in[s], l * (16 * UNITS // RING) + uses * 16 + 16 * (u // RING + 1))
                    act.wait_ge(unit_used, l * UNITS + off + (u + 1))
                    act.activation(w_hi[:, s, 0:width], raw[:, s, 0:width], ACT.Copy).then_inc(hi_done, 1)

                def his(first, last):
                    for u in range(first, last):
                        hi(u)

                def bank(b, use, j=None):
                    pair, t = b // 2, b % 2
                    if t == 0:
                        act.wait_ge(full[pair], l * FULL_COUNT[pair] + (0 if j is None else j)
                                   + full_count(pair, use))
                    else:
                        act.wait_ge(unit_used, l * UNITS + (0 if j is None else j * 8)
                                   + (RING + LAST_UNIT[pair][use] + 1))

                def stat(n):
                    act.wait_ge(r_done, l * NSTAT + (n + 1))
                    return rstd[:, n:n + 1]

                def square(n, src, scale=1.0):
                    if n:
                        act.wait_ge(ssq_done, l * NSTAT + n)
                    act.activation(junk[:, 0:src.shape[-1]], src, ACT.Square, scale=scale,
                                   accum_out=ssq[:, n:n + 1]).then_inc(ssq_done, 1)

                def hi_scaled(n, dst):
                    act.wait_ge(mul_done, l * 14 + mul_count(n))
                    w = dst.shape[1] * dst.shape[2]
                    act.activation(dst, tmp[:, n % 2, 0:w].rearrange("p (a b) -> p a b", a=dst.shape[1]),
                                   ACT.Copy).then_inc(tp_hi, 1)

                def hi_T(n, dst, off=0):
                    act.wait_ge(tp_full[n % 2], l * TP_FULL[n % 2] + off + tp_count(n))
                    w = dst.shape[1] * dst.shape[2]
                    act.activation(dst, tp[0:dst.shape[0], n % 2, 0:w].rearrange("p (a b) -> p a b", a=dst.shape[1]),
                                   ACT.Copy).then_inc(tp_hi, 1)

                def tokens(t):
                    return slice(t * P, (t + 1) * P)

                hi(0)
                for h in range(2):
                    hi_scaled(T_X + h, xT_hi[:, 4 * h:4 * h + 4, tokens(0)])
                his(1, 2)
                act.wait_ge(x_ready[0], l * 4 + 2)
                square(R_X, x[:, 0, :])
                his(2, 4)
                act.wait_ge(x_ready[1], l * 4 + 2)
                square(R_X + 1, x[:, 1, :])
                for h in range(2):
                    hi_scaled(T_X + 2 + h, xT_hi[:, 4 * h:4 * h + 4, tokens(1)])
                his(4, 6)
                bank(0, A_G)
                act.activation(sg[:, 0, :], acc[:, 0, :], ACT.Sigmoid, scale=stat(R_X)).then_inc(free[0], 1)
                his(6, 8)
                bank(1, A_G)
                act.activation(sg[:, 1, :], acc[:, 1, :], ACT.Sigmoid, scale=stat(R_X + 1)).then_inc(free[1], 1)
                his(8, 12)
                his(12, 16)
                for t in range(TOK):
                    bank(t, A_CQ)
                    square(R_CQ + t, acc[:, t, 0:Q_RANK], rstd[:, R_X + t:R_X + t + 1])
                    act.activation(cq[:, t, 0:Q_RANK], acc[:, t, 0:Q_RANK], ACT.Copy,
                                   scale=rstd[:, R_X + t:R_X + t + 1]).then_inc(free[t], 1)
                act.wait_ge(pad_zero, 1)
                for t in range(TOK):
                    n = T_HC + t
                    act.wait_ge(tp_full[n % 2], l * TP_FULL[n % 2] + tp_count(n))
                    act.activation(hcT[:, :, TAPS - 1 + t * P:TAPS - 1 + (t + 1) * P],
                                   tp[:, n % 2, :].rearrange("p (c n) -> p c n", c=CT),
                                   ACT.Copy).then_inc(tp_free[n % 2], 1)
                act.wait_ge(ang_ready, 1)
                act.activation(sin2[:, :, 0:HR], ang[:, 4], ACT.Sin, scale=-1.0)
                act.activation(sin2[:, :, HR:ROPE], ang[:, 4], ACT.Sin)
                act.activation(cos2[:, :, 0:HR], ang[:, 5], ACT.Sin)
                act.activation(cos2[:, :, HR:ROPE], ang[:, 5], ACT.Sin).then_inc(tables, 1)
                his(16, 20)
                for t in range(TOK):
                    bank(2 + t, B_CKV)
                    square(R_CKV + t, acc[:, 2 + t, 0:KV_RANK], rstd[:, R_X + t:R_X + t + 1])
                    act.activation(cq[:, t, Q_RANK:Q_RANK + CKV_W], acc[:, 2 + t, 0:CKV_W], ACT.Copy,
                                   scale=rstd[:, R_X + t:R_X + t + 1]).then_inc(free[2 + t], 1)
                for t in range(TOK):
                    hi_scaled(T_CQ + t, hT_hi[:, H_CQ:H_CQ + 3, tokens(t)])
                his(20, 24)
                for t in range(TOK):
                    bank(t, A_POOL)
                    act.activation(u_sb[:, t, :], acc[:, t, :], ACT.Copy,
                                   scale=rstd[:, R_X + t:R_X + t + 1]).then_inc(free[t], 1)
                for t in range(TOK):
                    hi_scaled(T_CKV + t, hT_hi[:, H_CKV:H_CKV + 2, tokens(t)])
                his(24, 27)
                def q_complete(t):
                    if t == 0:
                        act.wait_ge(misc_full[0], l * MISC_FULL[0] + 1)
                    else:
                        bank(3, B_Q)

                act.wait_ge(ssq_done, l * NSTAT + R_MIX)
                for t in range(TOK):
                    q_complete(t)
                    act.activation(q_sb[:, t, 0:384], acc[:, 2 + t, 0:384], ACT.Copy,
                                   scale=stat(R_CQ + t)).then_inc(free[2 + t], 1)
                act.wait_ge(ssq_done, l * NSTAT + R_MIX)
                for t in range(TOK):
                    q_complete(t)
                    act.activation(q_sb[:, t, 384:768], misc[:, t, 0:384], ACT.Copy,
                                   scale=rstd[:, R_CQ + t:R_CQ + t + 1]).then_inc(misc_free[t], 1)
                his(27, 29)
                for t in range(TOK):
                    bank(t, A_K)
                    act.activation(k_sb[:, t, :].rearrange("p (h d) -> p h d", h=HEADS)[:, :, 0:NOPE],
                                   acc[:, t, :].rearrange("p (h d) -> p h d", h=HEADS), ACT.Copy,
                                   scale=stat(R_CKV + t)).then_inc(k_nope, 1)
                    act.wait_ge(k_nope, l * TOK + (t + 1))
                    act.sem_inc(free[t], 1)
                for t in range(TOK):
                    bank(2 + t, B_V)
                    act.activation(v_sb[:, t, :], acc[:, 2 + t, :], ACT.Copy,
                                   scale=rstd[:, R_CKV + t:R_CKV + t + 1]).then_inc(free[2 + t], 1)
                for h in range(2):
                    act.wait_ge(misc_full[h], l * MISC_FULL[h] + (2 - h))
                    act.activation(hT_hi[:, H_CONV + 2 * h:H_CONV + 2 * h + 2, :],
                                   misc[:, h, :].rearrange("p (g n) -> p g n", g=2), ACT.Copy).then_inc(d_hi, 1)
                for n in range(4):
                    hh, t = n // 2, n % 2
                    hi_T(T_Q + n, hT_hi[0:QK, H_Q + 4 * hh:H_Q + 4 * hh + 4, tokens(t)])
                his(29, 30)
                for h in range(2):
                    hi_scaled(T_MT + h, hT_hi[:, H_POOL + 2 * h:H_POOL + 2 * h + 2, :])
                with act.Fori(0, 3) as j:
                    for g in range(2):
                        for i in range(4):
                            hi(U_GATE + 4 + 4 * g + i, j * 8, WU, j * 2)
                        for t in range(TOK):
                            bank(2 * g + t, ACC_GATE, j)
                            act.activation(gates[:, t, bass.ds(j * D + 512 * g, 512)], acc[:, 2 * g + t, :],
                                           ACT.Sigmoid, scale=rstd[:, R_X + t:R_X + t + 1]
                                           ).then_inc(free[2 * g + t], 1)
                for n in range(4):
                    hh, t = n // 2, n % 2
                    hi_T(T_K + n, xT_hi[0:QK, 4 * hh:4 * hh + 4, tokens(t)])
                his(54, 55)
                act.wait_ge(centred, l + 1)
                act.activation(sq[:, :, :], xc, ACT.Square).then_inc(sq_done, 1)

                for n in range(STEPS + 2):
                    u = {**{k: U_POOLO + k for k in range(1, 7)}, 9: U_POOLO + 7}.get(n)
                    if u:
                        hi(u + RING)
                    if 1 <= n <= STEPS:
                        m = n - 1
                        use = T_P + m
                        act.wait_ge(tp_full[use % 2], l * TP_FULL[use % 2] + tp_count(use))
                        if m >= 2:
                            act.wait_ge(pv_done, l * STEPS + (m - 1))
                        blocks = 2 * (m % 2 + 1)
                        act.activation(pT[:, m % 2, 0:blocks, :],
                                       tp[:, use % 2, 0:blocks * P].rearrange("p (b n) -> p b n", b=blocks),
                                       ACT.Copy).then_inc(tp_free[use % 2], 1)
                    if n < STEPS:
                        keys = (n % 2 + 1) * P
                        act.wait_ge(nm_done, l * STEPS + (n + 1))
                        for i in range(2):
                            e = act.activation(probs[:, n % 2, i, 0:keys], misc[:, n % 2, i * keys:(i + 1) * keys],
                                               ACT.Exp, scale=SCALE, bias=nmx[:, n % 2, i:i + 1],
                                               accum_out=rsum[:, n % 2, i:i + 1])
                        e.then_inc(exp_done, 1)
                    if n == 2:
                        act.wait_ge(par_ready, l + 1)
                        act.wait_ge(misc_free[1], l * (M_USES // 2) + (M_VAR // 2 + 2))
                        for c in range(CT):
                            act.activation(sq[:, c, :], xc[:, c, :], ACT.Silu, scale=par[:, C_LG + c:C_LG + c + 1],
                                           bias=par[:, C_LB + c:C_LB + c + 1]).then_inc(csilu, 1)
                        act.wait_ge(csilu, l * CT + CT)
                        act.activation(hT_hi[:, H_CONV:H_CONV + CT, :], sq[:, :, :], ACT.Copy).then_inc(conv_hi, 1)
                for t in range(TOK):
                    hi_T(T_O + t, hT_hi[:, H_O:H_O + 4, tokens(t)])
                his(62, 65)
                for t in range(TOK):
                    hi_T(T_M + t, xT_hi[:, 0:4, tokens(t)])
                his(65, 68)
                for t in range(TOK):
                    hi_T(T_M + 2 + t, xT_hi[:, 4:8, tokens(t)])
                his(68, 70)

                def post_square(n, t, use):
                    if t == 0:
                        act.wait_ge(wide_full, l * 2 + (1 if use == ACC_MIX else 2))
                    else:
                        act.wait_ge(unit_used, l * UNITS + (RING + (U_FFN if use == ACC_MIX else UNITS)))
                    square(n, acc[:, 2 * t:2 * t + 2, :].rearrange("p a n -> p (a n)"))

                post_square(R_MIX, 0, ACC_MIX)
                his(70, 73)
                for h in range(2):
                    hi_scaled(T_F + h, xT_hi[:, 4 * h:4 * h + 4, tokens(0)])
                post_square(R_MIX + 1, 1, ACC_MIX)
                his(73, 74)
                act.wait_ge(x_ready[0], l * 4 + 4)
                square(R_F, x[:, 0, :])
                for h in range(2):
                    hi_scaled(T_F + 2 + h, xT_hi[:, 4 * h:4 * h + 4, tokens(1)])
                act.wait_ge(x_ready[1], l * 4 + 4)
                square(R_F + 1, x[:, 1, :])
                his(74, 78)
                for t in range(TOK):
                    bank(t, ACC_FFN)
                    act.activation(sg[:, t, :], acc[:, t, :], ACT.Silu, scale=stat(R_F + t)
                                   ).then_inc(free[t], 1)
                his(78, 82)
                with act.Fori(0, FULL_CHUNKS - 1) as j:
                    for i in range(4):
                        hi(U_FFN + 12 + i, j * 8, WU, j * 2)
                    for t in range(TOK):
                        bank(t, ACC_FFN + 1, j)
                        act.wait_ge(free[2 + t], l * ACC_USES + j + (ACC_FFN + 2))
                        act.activation(sg[:, t, :], acc[:, t, :], ACT.Silu,
                                       scale=rstd[:, R_F + t:R_F + t + 1]).then_inc(free[t], 1)
                    for t in range(TOK):
                        act.wait_ge(tp_full[t], l * TP_FULL[t] + j + tp_count(T_H + t))
                        act.activation(hT_hi[:, bass.ds(j * 4, 4), tokens(t)],
                                       tp[:, t, :].rearrange("p (a b) -> p a b", a=4), ACT.Copy).then_inc(tp_hi, 1)
                    for i in range(4):
                        hi(U_FFN + 16 + i, j * 8, WU, j * 2)
                his(114, 116)
                for t in range(TOK):
                    bank(t, ACC_LAST)
                    act.wait_ge(free[2 + t], l * ACC_USES + (ACC_LAST + 1))
                    act.activation(sg[:, t, 0:LAST_W], acc[:, t, 0:LAST_W], ACT.Silu,
                                   scale=rstd[:, R_F + t:R_F + t + 1]).then_inc(free[t], 1)
                for t in range(TOK):
                    hi_T(T_HLAST - 2 + t, hT_hi[:, FT - 6:FT - 2, tokens(t)])
                his(116, 120)
                for t in range(TOK):
                    hi_T(T_HLAST + t, hT_hi[:, FT - 2:FT, tokens(t)])
                his(120, 136)
                for t in range(TOK):
                    post_square(R_DOWN + t, t, ACC_DOWN)
                act.preload_act_table(ACT.Sigmoid)

        @block.vector
        def _(dve):
            def f(ap):
                return ap.bitcast(F32)

            dve.sem_inc(lo_done, RING)
            dve.sem_inc(gain_used, 1)
            dve.memset(hcT[:, :, 0:TAPS - 1], 0.0).then_inc(pad_zero, 1)

            dve.wait_ge(const_in, 48)

            with dve.Fori(0, LAYERS) as l:
                steps = [0]

                def step(ins):
                    steps[0] += 1
                    ins.then_inc(dve_step, 1)
                    dve.wait_ge(dve_step, l * DVE_STEPS + steps[0])

                def lo(u, off=0, width=None):
                    s = u % RING
                    width = width or unit_width(u)
                    dve.wait_ge(hi_done, l * UNITS + off + (u + 1))
                    dve.tensor_tensor(w_lo[:, s, 0:width], raw[:, s, 0:width], f(w_hi[:, s, 0:width]),
                                      ALU.subtract).then_inc(lo_done, 1)

                def los(first, last):
                    for u in range(first, last):
                        lo(u)

                def tokens(t):
                    return slice(t * P, (t + 1) * P)

                def split3(ap, a):
                    return ap.rearrange("p (a b) -> p a b", a=a)

                def scaled(n, tiles, width, col):
                    if n == T_MT + 1:
                        dve.wait_ge(unit_used, l * UNITS + (RING + U_MT + 1))
                    else:
                        dve.wait_ge(tp_full[n % 2], l * TP_FULL[n % 2] + tp_count(n))
                    g = par[:, col:col + tiles].unsqueeze(2).to_broadcast((P, tiles, width))
                    dve.tensor_tensor(split3(tmp[:, n % 2, 0:tiles * width], tiles),
                                      split3(tp[:, n % 2, 0:tiles * width], tiles), g, ALU.mult
                                      ).then_inc(mul_done, 1)

                def lo_scaled(n, dst, src_hi):
                    dve.wait_ge(tp_hi, l * 40 + hi_count(n))
                    a = dst.shape[1]
                    dve.tensor_tensor(dst, split3(tmp[:, n % 2, 0:a * dst.shape[2]], a), f(src_hi),
                                      ALU.subtract).then_inc(tp_free[n % 2], 1)

                def lo_T(n, dst, src_hi):
                    dve.wait_ge(tp_hi, l * 40 + hi_count(n))
                    a = dst.shape[1]
                    dve.tensor_tensor(dst, split3(tp[0:dst.shape[0], n % 2, 0:a * dst.shape[2]], a), f(src_hi),
                                      ALU.subtract).then_inc(tp_free[n % 2], 1)

                def x_parts(n0, t, col, between=None):
                    for h in range(2):
                        scaled(n0 + 2 * t + h, 4, P, col + 4 * h)
                    if between is not None:
                        lo(between)
                    for h in range(2):
                        k = slice(4 * h, 4 * h + 4)
                        lo_scaled(n0 + 2 * t + h, xT_lo[:, k, tokens(t)], xT_hi[:, k, tokens(t)])

                def bank(b, use, j=None):
                    pair, t = b // 2, b % 2
                    if t == 0:
                        dve.wait_ge(full[pair], l * FULL_COUNT[pair] + (0 if j is None else j)
                                   + full_count(pair, use))
                    else:
                        dve.wait_ge(unit_used, l * UNITS + (0 if j is None else j * 8)
                                   + (RING + LAST_UNIT[pair][use] + 1))

                def rope(dst, src, t, heads):
                    n = src.shape[1]
                    c = cos2[:, t, :].unsqueeze(1).to_broadcast((P, n, ROPE))
                    s0 = sin2[:, t, 0:HR].unsqueeze(1).to_broadcast((P, n, HR))
                    s1 = sin2[:, t, HR:ROPE].unsqueeze(1).to_broadcast((P, n, HR))
                    a, b = split3(rope_a[:, 0:n * ROPE], n), split3(rope_b[:, 0:n * ROPE], n)
                    dve.tensor_tensor(a, src, c, ALU.mult)
                    dve.tensor_tensor(b[:, :, 0:HR], src[:, :, HR:ROPE], s0, ALU.mult)
                    step(dve.tensor_tensor(b[:, :, HR:ROPE], src[:, :, 0:HR], s1, ALU.mult))
                    if n < heads:
                        a, b = a.to_broadcast((P, heads, ROPE)), b.to_broadcast((P, heads, ROPE))
                    return dve.tensor_tensor(dst, a, b, ALU.add)

                step(dve.tensor_copy(par[:, :], par2[:, bass.ds(l, 1), :].rearrange("p a n -> p (a n)")))
                dve.sem_inc(par_ready, 1)
                x_parts(T_X, 0, C_PRE, between=0)
                los(1, 4)
                x_parts(T_X, 1, C_PRE)
                los(4, 12)
                for t in range(TOK):
                    bank(2 + t, B_A)
                    dve.wait_ge(free[t], l * ACC_USES + (A_G + 2))
                    dve.wait_ge(r_done, l * NSTAT + (R_X + t + 1))
                    dve.scalar_tensor_tensor(out=hc[:, t, :], in0=acc[:, 2 + t, :], scalar=rstd[:, R_X + t:R_X + t + 1],
                                             in1=sg[:, t, :], op0=ALU.mult, op1=ALU.mult).then_inc(free[2 + t], 1)
                los(12, 20)
                for t in range(TOK):
                    scaled(T_CQ + t, 3, P, C_QN)
                for t in range(TOK):
                    lo_scaled(T_CQ + t, hT_lo[:, H_CQ:H_CQ + 3, tokens(t)], hT_hi[:, H_CQ:H_CQ + 3, tokens(t)])
                dve.wait_ge(tables, l + 1)
                for t in range(TOK):
                    dve.wait_ge(free[2 + t], l * ACC_USES + (B_CKV + 2))
                    k0 = Q_RANK + KV_RANK
                    if t == 1:
                        dve.wait_ge(k_roped, l * TOK + 1)
                    rope(split3(k_sb[:, t, :], HEADS)[:, :, NOPE:QK], cq[:, t, k0:k0 + ROPE].unsqueeze(1), t, HEADS
                         ).then_inc(k_roped, 1)
                los(20, 24)
                for t in range(TOK):
                    scaled(T_CKV + t, 2, P, C_KVN)
                for t in range(TOK):
                    lo_scaled(T_CKV + t, hT_lo[:, H_CKV:H_CKV + 2, tokens(t)], hT_hi[:, H_CKV:H_CKV + 2, tokens(t)])
                los(24, 29)
                for t in range(TOK):
                    dve.wait_ge(free[2 + t], l * ACC_USES + (B_Q + 2))
                    dve.wait_ge(misc_free[t], l * (M_USES // 2) + 2)
                    if t == 1:
                        dve.wait_ge(q_roped, l * TOK + 1)
                    qr = split3(q_sb[:, t, :], HEADS)[:, :, NOPE:QK]
                    rope(qr, qr, t, HEADS).then_inc(q_roped, 1)
                for h in range(2):
                    dve.wait_ge(d_hi, l * 2 + (h + 1))
                    k = slice(H_CONV + 2 * h, H_CONV + 2 * h + 2)
                    dve.tensor_tensor(hT_lo[:, k, :], split3(misc[:, h, :], 2), f(hT_hi[:, k, :]),
                                      ALU.subtract).then_inc(misc_free[h], 1)
                for n in range(4):
                    hh, t = n // 2, n % 2
                    k = slice(H_Q + 4 * hh, H_Q + 4 * hh + 4)
                    lo_T(T_Q + n, hT_lo[0:QK, k, tokens(t)], hT_hi[0:QK, k, tokens(t)])
                los(29, 30)
                for h in range(2):
                    scaled(T_MT + h, 2, SEQ, C_PS + 2 * h)
                for h in range(2):
                    k = slice(H_POOL + 2 * h, H_POOL + 2 * h + 2)
                    lo_scaled(T_MT + h, hT_lo[:, k, :], hT_hi[:, k, :])

                done0 = steps[0]
                with dve.Fori(0, 3) as j:
                    def tap(k, even, odd):
                        src = hcT[:, bass.ds(j, 1), k:k + SEQ].rearrange("p a n -> p (a n)")
                        w = par[:, bass.ds(j * TAPS + (C_CW + k), 1)]
                        if k == 0:
                            dve.wait_ge(conv_pool, l * CT + j + 1)
                        if k >= 2:
                            dve.wait_ge(dve_step, l * DVE_STEPS + j * (OWN + 1) + (done0 + k - 1))
                        if k == 1:
                            ins = dve.tensor_scalar(odd, src, w, None, ALU.mult)
                        else:
                            s = even if k % 2 == 0 else odd
                            ins = dve.scalar_tensor_tensor(out=s, in0=src, scalar=w, in1=s, op0=ALU.mult, op1=ALU.add)
                        ins.then_inc(dve_step, 1)

                    even = cacc[:, bass.ds(j, 1), :].rearrange("p a n -> p (a n)")
                    odd = cacc_odd[:, :]
                    for i in range(8):
                        lo(U_GATE + 4 + i, j * 8, WU)
                        for k in range(OWN * i // 8, OWN * (i + 1) // 8):
                            tap(k, even, odd)
                    dve.wait_ge(dve_step, l * DVE_STEPS + j * (OWN + 1) + (done0 + OWN))
                    dve.tensor_tensor(even, even, odd, ALU.add).then_inc(conv_dve, 1)
                    dve.wait_ge(conv_dve, l * 3 + j + 1)
                    dve.sem_inc(dve_step, 1)
                steps[0] += 3 * (OWN + 1)

                for n in range(4):
                    hh, t = n // 2, n % 2
                    k = slice(4 * hh, 4 * hh + 4)
                    lo_T(T_K + n, xT_lo[0:QK, k, tokens(t)], xT_hi[0:QK, k, tokens(t)])
                    if n == 1:
                        dve.wait_ge(misc_full[0], l * MISC_FULL[0] + 3)
                        dve.tensor_tensor(xc, cacc[:, :, :], misc[:, 0:1, 0:SEQ].to_broadcast((P, CT, SEQ)),
                                          ALU.subtract).then_inc(misc_free[0], 1)
                        dve.wait_ge(misc_free[0], l * (M_USES // 2) + (M_MEAN // 2 + 2))
                        dve.sem_inc(centred, 1)
                los(54, 55)
                dve.wait_ge(misc_full[1], l * MISC_FULL[1] + 2)
                dve.tensor_scalar(cvar[:, :], misc[:, 1, 0:TOK], EPS, None, ALU.add).then_inc(var_in, 1)

                def gate(branch, h, t, use):
                    b = 2 * h + t
                    bank(b, use)
                    g = gates[:, t, branch * D + 512 * h:branch * D + 512 * (h + 1)]
                    return dve.tensor_tensor(g, g, acc[:, b, :], ALU.mult)

                for n in range(STEPS + 2):
                    u = {**{k: U_POOLO + k for k in range(1, 7)}, 9: U_POOLO + 7}.get(n)
                    if n == 1:
                        dve.wait_ge(spread, l + 1)
                        dve.tensor_tensor(xc, xc, misc[:, 1:2, 0:SEQ].to_broadcast((P, CT, SEQ)),
                                          ALU.mult).then_inc(misc_free[1], 1)
                    if n >= 2:
                        m = n - 2
                        hp, t = m // 2, m % 2
                        dve.wait_ge(pv_done, l * STEPS + (m + 1))
                        step(dve.reciprocal(rinv[:, m % 2, :], rsum[:, m % 2, :]))
                        dve.tensor_tensor(split3(o_sb[:, t, 2 * hp * VDIM:2 * (hp + 1) * VDIM], 2),
                                          split3(misc[:, m % 2, 0:2 * VDIM], 2),
                                          rinv[:, m % 2, :].unsqueeze(2).to_broadcast((P, 2, VDIM)),
                                          ALU.mult).then_inc(misc_free[m % 2], 1)
                    if n < STEPS:
                        t = n % 2
                        keys = (t + 1) * P
                        s = split3(misc[:, n % 2, 0:2 * keys], 2)
                        dve.wait_ge(s_done, l * STEPS + (n + 1))
                        step(dve.tensor_tensor(s[:, :, t * P:keys], s[:, :, t * P:keys],
                                               mask.unsqueeze(1).to_broadcast((P, 2, P)), ALU.add))
                        step(dve.tensor_reduce(mx[:, n % 2, :], s, AX_X, ALU.max))
                        dve.tensor_scalar(nmx[:, n % 2, :], mx[:, n % 2, :], -SCALE, None, ALU.mult
                                          ).then_inc(nm_done, 1)
                    if n == 0:
                        dve.wait_ge(cstd, l + 1)
                        for t in range(TOK):
                            dve.tensor_scalar(rope_a[:, tokens(t)], ident, crstd[:, t:t + 1], float(CONV),
                                              ALU.mult, ALU.mult).then_inc(diag_done, 1)
                    if u:
                        lo(u + RING)
                    if n == 2:
                        dve.wait_ge(conv_hi, l + 1)
                        dve.tensor_tensor(hT_lo[:, H_CONV:H_CONV + CT, :], sq[:, :, :],
                                          f(hT_hi[:, H_CONV:H_CONV + CT, :]), ALU.subtract).then_inc(conv_lo, 1)
                    if n in (2, 4):
                        h = n // 2 - 1
                        for t in range(TOK):
                            gate(2, h, t, ACC_POOLO).then_inc(free[2 * h + t], 1)
                    if n == 6:
                        for t in range(TOK):
                            gate(1, 0, t, ACC_CONVO).then_inc(free[t], 1)
                for t in range(TOK):
                    k = slice(H_O, H_O + 4)
                    lo_T(T_O + t, hT_lo[:, k, tokens(t)], hT_hi[:, k, tokens(t)])
                for t in range(TOK):
                    gate(1, 1, t, ACC_CONVO).then_inc(free[2 + t], 1)

                def merge(h):
                    for t in range(TOK):
                        gate(0, h, t, ACC_ATTNO).then_inc(free[2 * h + t], 1)
                    for t in range(TOK):
                        dve.wait_ge(free[2 * h + t], l * ACC_USES + (ACC_ATTNO + 2))
                        dve.wait_ge(summed, l * 4 + (2 * h + t + 1))
                        g = gates[:, t, 512 * h:512 * (h + 1)]
                        dve.tensor_tensor(g, g, gates[:, t, 2 * D + 512 * h:2 * D + 512 * (h + 1)],
                                          ALU.add).then_inc(merged, 1)

                los(62, 64)
                merge(0)
                los(64, 65)
                for t in range(TOK):
                    lo_T(T_M + t, xT_lo[:, 0:4, tokens(t)], xT_hi[:, 0:4, tokens(t)])
                merge(1)
                los(65, 68)
                for t in range(TOK):
                    lo_T(T_M + 2 + t, xT_lo[:, 4:8, tokens(t)], xT_hi[:, 4:8, tokens(t)])
                los(68, 70)

                def post_norm(n, t, use, which):
                    dve.wait_ge(r_done, l * NSTAT + (n + 1))
                    dve.wait_ge(gain_in, l * 32 + 16 * (which + 1))
                    y = gates[:, t, D:2 * D]
                    for h in range(2):
                        dve.scalar_tensor_tensor(out=y[:, 512 * h:512 * (h + 1)], in0=acc[:, 2 * t + h, :],
                                                 scalar=rstd[:, n:n + 1], in1=gain[:, 512 * h:512 * (h + 1)],
                                                 op0=ALU.mult, op1=ALU.mult).then_inc(free[2 * t + h], 1)
                    for h in range(2):
                        dve.wait_ge(free[2 * t + h], l * ACC_USES + (use + 2))
                        if h == 1:
                            dve.sem_inc(gain_used, 1)
                        k = slice(512 * h, 512 * (h + 1))
                        dve.tensor_tensor(x[:, t, k], x[:, t, k], y[:, k], ALU.add).then_inc(x_ready[t], 1)

                post_norm(R_MIX, 0, ACC_MIX, 0)
                los(70, 71)
                x_parts(T_F, 0, C_PREF)
                los(71, 73)
                post_norm(R_MIX + 1, 1, ACC_MIX, 0)
                los(73, 74)
                x_parts(T_F, 1, C_PREF)
                los(74, 82)

                def hidden(t, use, width, j=None):
                    bank(2 + t, use, j)
                    dve.wait_ge(free[t], l * ACC_USES + (0 if j is None else j) + (use + 2))
                    n = R_F + t
                    dve.wait_ge(r_done, l * NSTAT + (n + 1))
                    dve.scalar_tensor_tensor(out=hid[:, t, 0:width], in0=acc[:, 2 + t, 0:width],
                                             scalar=rstd[:, n:n + 1], in1=sg[:, t, 0:width],
                                             op0=ALU.mult, op1=ALU.mult).then_inc(free[2 + t], 1)

                for t in range(TOK):
                    hidden(t, ACC_FFN, 512)
                with dve.Fori(0, FULL_CHUNKS - 1) as j:
                    for i in range(4):
                        lo(U_FFN + 12 + i, j * 8, WU)
                    for t in range(TOK):
                        dve.wait_ge(tp_hi, l * 40 + j * 2 + (hi_count(T_H) + t))
                        dve.tensor_tensor(hT_lo[:, bass.ds(j * 4, 4), tokens(t)], split3(tp[:, t, :], 4),
                                          f(hT_hi[:, bass.ds(j * 4, 4), tokens(t)]), ALU.subtract
                                          ).then_inc(tp_free[t], 1)
                    for i in range(4):
                        lo(U_FFN + 16 + i, j * 8, WU)
                    for t in range(TOK):
                        hidden(t, ACC_FFN + 1, 512, j)
                los(114, 116)
                for t in range(TOK):
                    lo_T(T_HLAST - 2 + t, hT_lo[:, FT - 6:FT - 2, tokens(t)], hT_hi[:, FT - 6:FT - 2, tokens(t)])
                los(116, 118)
                for t in range(TOK):
                    hidden(t, ACC_LAST, LAST_W)
                los(118, 120)
                for t in range(TOK):
                    lo_T(T_HLAST + t, hT_lo[:, FT - 2:FT, tokens(t)], hT_hi[:, FT - 2:FT, tokens(t)])
                los(120, 136)
                for t in range(TOK):
                    post_norm(R_DOWN + t, t, ACC_DOWN, 1)
                assert steps[0] == DVE_STEPS, steps[0]

        @block.gpsimd
        def _(pool):
            count = [0]
            pool.memset(half[:, :], -0.5).then_inc(pool_step, 1)
            pool.wait_ge(pool_step, 1)
            for t in range(TOK):
                pool.wait_ge(x_in[t], 16)
                pool.sem_inc(x_ready[t], 2)
            pool.wait_ge(const_in, 48)

            linked = [0]

            def link(ins):
                linked[0] += 1
                ins.then_inc(setup, 1)
                pool.wait_ge(setup, linked[0])

            link(pool.tensor_copy(pos_f[:, :], pos_i[:, :]))
            freq = const[:, K_FREQ:K_FREQ + HR]
            for t in range(TOK):
                link(pool.tensor_scalar(ang[:, 0, t, :], freq, pos_f[:, t:t + 1], None, ALU.mult))
            for which, shift in ((4, 0.0), (5, 0.25)):
                turns, back, part = ang[:, 1], ang[:, 2], ang[:, 3]
                link(pool.tensor_scalar(turns, ang[:, 0], 1.0 / TWO_PI, shift, ALU.mult, ALU.add))
                link(pool.tensor_scalar(turns, turns, ROUND, None, ALU.add))
                link(pool.tensor_scalar(turns, turns, ROUND, None, ALU.subtract))
                src = ang[:, 0]
                for c in TURN:
                    link(pool.tensor_scalar(part, turns, c, None, ALU.mult))
                    link(pool.tensor_tensor(back, src, part, ALU.subtract))
                    src = back
                link(pool.tensor_scalar(back, back, shift * TWO_PI, PI_BELOW, ALU.add, ALU.min))
                link(pool.tensor_scalar(ang[:, which], back, -PI_BELOW, None, ALU.max))
            pool.sem_inc(ang_ready, 1)
            pool.dma_start(const[:, K_BAND:NCONST], const_d[:, K_BAND:NCONST]).then_inc(band_in, 16)
            POOL_STEPS = (CT - 1) * (2 * SHARE - 1) + 2 * TAPS - 1

            with pool.Fori(0, LAYERS) as l:
                def before_scalar():
                    pool.sem_inc(pool_went, 1)

                def norm(n):
                    pool.wait_ge(ssq_done, l * NSTAT + (n + 1))
                    before_scalar()
                    pool.tensor_scalar(mean2[:, n:n + 1], ssq[:, n:n + 1], 1.0 / STAT_WIDTH[n], EPS,
                                       ALU.mult, ALU.add).then_inc(mean_done, 1)
                    pool.wait_ge(mean_done, l * NSTAT + (n + 1))
                    pool.tensor_tensor(rstd[:, n:n + 1], mean2[:, n:n + 1], half[:, :], ALU.pow
                                       ).then_inc(r_done, 1)

                for n in range(R_MIX):
                    norm(n)
                for t in range(TOK):
                    pool.wait_ge(tp_free[(T_HC + t) % 2], l * (T_USES // 2) + ((T_HC + t) // 2 + 2))
                pool.wait_ge(par_ready, l + 1)
                before_scalar()
                done = 1

                def chained(ins, done):
                    ins.then_inc(pool_step, 1)
                    pool.wait_ge(pool_step, l * POOL_STEPS + done)

                for c in range(CT):
                    first = OWN if c < CT - 1 else 0
                    for k in range(first, TAPS):
                        src = hcT[:, c, k:k + SEQ]
                        w = par[:, C_CW + c * TAPS + k:C_CW + c * TAPS + k + 1]
                        if k == first:
                            done += 1
                            chained(pool.tensor_scalar(cacc[:, c, :], src, w, par[:, C_CB + c:C_CB + c + 1],
                                                       ALU.mult, ALU.add), done)
                        else:
                            done += 2
                            chained(pool.tensor_scalar(cprod[:, :], src, w, None, ALU.mult), done - 1)
                            chained(pool.tensor_tensor(cacc[:, c, :], cacc[:, c, :], cprod[:, :], ALU.add), done)
                        before_scalar()
                    pool.sem_inc(conv_pool, 1)
                assert done == POOL_STEPS + 1
                pool.wait_ge(var_in, l + 1)
                pool.tensor_tensor(crstd[:, :], cvar[:, :], half[:, :].to_broadcast((P, TOK)), ALU.pow
                                   ).then_inc(cstd, 1)
                for h in range(2):
                    for t in range(TOK):
                        b = 2 * h + t
                        pool.wait_ge(free[b], l * ACC_USES + (ACC_CONVO + 2))
                        s = gates[:, t, 2 * D + 512 * h:2 * D + 512 * (h + 1)]
                        pool.tensor_tensor(s, s, gates[:, t, D + 512 * h:D + 512 * (h + 1)], ALU.add
                                           ).then_inc(summed, 1)
                for n in range(R_MIX, NSTAT):
                    norm(n)


def unit_width(u):
    if U_CQ <= u < U_CKV:
        return 2 * Q_RANK
    if U_CKV <= u < U_POOL:
        return 2 * CKV_W
    if U_Q <= u < U_K:
        return HEADS * QK
    return 512 if u == U_MT else WU


def weight_stream(a):
    out = np.zeros((LAYERS, UNITS, P, WU), np.float32)

    def put(u0, w, per):
        L, K, n = w.shape
        t = w.reshape(L, K // (P * per), per, P, n).transpose(0, 1, 3, 2, 4)
        out[:, u0:u0 + K // (P * per), :, 0:per * n] = t.reshape(L, K // (P * per), P, per * n)

    w = a["w_in"]
    edges = np.cumsum([0, Q_RANK, KV_RANK + ROPE, CONV, CONV, 512, 3 * D])
    c_q, c_kv, conv_a, conv_g, pool, gate = (w[:, :, edges[i]:edges[i + 1]] for i in range(6))
    put(U_G, conv_g, 2)
    put(U_A, conv_a, 2)
    put(U_CQ, c_q, 2)
    put(U_CKV, c_kv, 2)
    put(U_POOL, pool, 2)
    put(U_Q, a["w_uq"], 1)
    put(U_K, a["w_uk"], 2)
    put(U_V, a["w_uv"], 2)
    pw = a["pool_w"]
    put(U_MT, pw.transpose(0, 2, 1, 3).reshape(LAYERS, P, 4 * P), 1)
    for g in range(6):
        put(U_GATE + 4 * g, gate[:, :, 512 * g:512 * (g + 1)], 2)
    for u0, name in ((U_POOLO, "w_pool_o"), (U_CONVO, "w_conv_o"), (U_ATTNO, "w_attn_o")):
        for g in range(2):
            put(u0 + 2 * g, a[name][:, :, 512 * g:512 * (g + 1)], 2)
    put(U_MIX, a["w_mix_o"], 1)
    for g in range(FULL_CHUNKS):
        for i, name in enumerate(("w_gate", "w_up")):
            put(U_FFN + 8 * g + 4 * i, a[name][:, :, 512 * g:512 * (g + 1)], 2)
    for i, name in enumerate(("w_gate", "w_up")):
        put(U_LAST + 2 * i, a[name][:, :, 512 * FULL_CHUNKS:], 4)
    put(U_DOWN, a["w_down"], 1)
    return out.reshape(LAYERS * UNITS * P, WU)


def parameters(a):
    cols = [a[name].reshape(LAYERS, -1, P).transpose(2, 0, 1)
            for name in ("mix_norm_pre", "ffn_norm_pre", "q_norm", "kv_norm", "pool_scale",
                         "conv_b", "conv_ln_g", "conv_ln_b")]
    cw = a["conv_w"].reshape(LAYERS, TAPS, CT, P).transpose(3, 0, 2, 1).reshape(P, LAYERS, CT * TAPS)
    return np.ascontiguousarray(np.concatenate(cols + [cw], axis=2))


def constants():
    c = np.zeros((P, NCONST), np.float32)
    c[:, K_ID:K_ID + P] = np.eye(P)
    c[:, K_ONE:K_ONE + P] = 1.0 / CONV
    c[:, K_MASK:K_MASK + P] = np.triu(np.full((P, P), MASKED, np.float32), 1)
    s, t = np.arange(SEQ)[:, None], np.arange(SEQ)[None, :]
    for g, w in enumerate(POOL_WINDOWS):
        band = np.where((s <= t) & (s > t - w), 1.0 / np.minimum(t + 1, w), 0.0) - (s == t)
        c[:, K_BAND + g * BANDW:K_BAND + g * BANDW + SEQ] = band[0:P]
        c[:, K_BAND + g * BANDW + SEQ:K_BAND + (g + 1) * BANDW] = band[P:, P:]
    c[:, K_FREQ:K_FREQ + HR] = np.power(np.float32(10000.0),
                                        -np.arange(0, ROPE, 2, dtype=np.float32) / np.float32(ROPE))
    return c


def kernel(**inputs):
    import concourse.bacc as bacc
    from concourse.bass_utils import run_bass_kernel_spmd

    a = {k: np.asarray(v) for k, v in inputs.items()}
    arrays = {
        "weights": weight_stream(a),
        "params": parameters(a),
        "consts": constants(),
        "gains": np.ascontiguousarray(np.stack([a["mix_norm_post"], a["ffn_norm_post"]], 1).reshape(2 * LAYERS, D)),
        "x_rows": np.ascontiguousarray(a["x"].reshape(SEQ, D)),
        "pos": np.ascontiguousarray(a["positions"].reshape(TOK, P).T),
    }
    nc = bacc.Bacc("TRN2", target_bir_lowering=False, num_devices=1)
    args = [nc.dram_tensor(name, v.shape, mybir.dt.from_np(v.dtype), kind="ExternalInput").ap()
            for name, v in arrays.items()]
    out = nc.dram_tensor("out_rows", (SEQ, D), F32, kind="ExternalOutput").ap()
    build(nc, *args, out)
    r = run_bass_kernel_spmd(nc, [arrays], core_ids=[0])
    return r.results[0]["out_rows"].reshape(1, SEQ, D)
```

```python
from contextlib import ExitStack

import concourse.bass as bass
import numpy as np
from concourse import mybir

F32 = mybir.dt.float32
F32R = mybir.dt.float32r
I32 = mybir.dt.int32
ALU = mybir.AluOpType
ACT = mybir.ActivationFunctionType
AX_X = mybir.AxisListType.X

P = 128
LAYERS, SEQ, D = 2, 256, 1024
TOK = SEQ // P
KD = D // P
HEADS, NOPE, ROPE, VDIM = 8, 64, 32, 64
QK = NOPE + ROPE
HR = ROPE // 2
Q_RANK, KV_RANK = 384, 256
CONV, TAPS = 512, 31
CT = CONV // P
POOL_WINDOWS = (2, 4, 8, 16)
D_FF = 2816
FT = D_FF // P
EPS = 1e-6
SCALE = float(1.0 / np.sqrt(QK))
MASKED = -3.0e38
TWO_PI = 6.283185307179586
PI_BELOW = 3.1415925
ROUND = 12582912.0
TURN = (6.28125, 0.0019350051879882812, 3.01991598196e-07)

WU = 1024
RING = 4
POOL_UNITS = (70, 71, 73)
(U_G, U_A, U_CQ, U_CKV, U_Q, U_POOL, U_K, U_V, U_MT, U_GATE, U_POOLO, U_CONVO, U_ATTNO, U_MIX, U_FFN,
 U_LAST, U_DOWN, UNITS) = (0, 4, 8, 12, 16, 19, 23, 24, 25, 26, 50, 54, 58, 62, 70, 110, 114, 136)
CKV_W = KV_RANK + ROPE
FULL_CHUNKS = 5
LAST_W = D_FF - 512 * FULL_CHUNKS

A_G, A_CQ, A_Q, A_K = 0, 1, 2, 3
B_A, B_CKV, B_POOL, B_V = 0, 1, 2, 3
ACC_GATE, ACC_POOLO, ACC_CONVO, ACC_ATTNO, ACC_MIX, ACC_FFN, ACC_LAST, ACC_DOWN, ACC_USES = (
    4, 7, 8, 9, 10, 11, 16, 17, 18)
T_X, T_HC, T_CQ, T_CKV, T_Q, T_MT, T_K, T_P, T_M, T_F, T_H, T_HLAST, T_USES = (
    0, 4, 6, 8, 10, 14, 16, 20, 30, 34, 38, 48, 50)
T_O0, T_O1 = T_P + 4, T_P + 9
M_Q, M_D, M_MEAN, M_VAR, M_S, M_USES = 0, 2, 4, 5, 6, 14
R_X, R_CQ, R_CKV, R_MIX, R_F, R_DOWN, NSTAT = 0, 2, 4, 6, 8, 10, 12
STAT_WIDTH = [D, D, Q_RANK, Q_RANK, KV_RANK, KV_RANK, D, D, D, D, D, D]
C_PRE, C_PREF, C_QN, C_KVN, C_PS, C_CB, C_LG, C_LB, C_CW, NPAR = 0, 8, 16, 19, 21, 25, 29, 33, 37, 161
K_ID, K_FREQ, K_ONE, K_MASK, K_BAND, NCONST = 0, 128, 144, 272, 400, 1936
BANDW = SEQ + P
H_CKV, H_CQ, H_O, H_CONV, H_POOL, H_Q = 3, 0, 0, 5, 9, 13
STEPS = HEADS // 2 * TOK
SHARE = 6
OWN = TAPS - SHARE
DVE_STEPS = 107


LAST_UNIT = (
    {A_G: 3, A_CQ: 11, A_Q: 18, A_K: 23, ACC_GATE: 29, ACC_POOLO: 51, ACC_CONVO: 55, ACC_ATTNO: 60,
     ACC_FFN: 73, ACC_FFN + 1: 81, ACC_LAST: 111},
    {B_A: 7, B_CKV: 15, B_POOL: 22, B_V: 24, ACC_GATE: 33, ACC_POOLO: 53, ACC_CONVO: 57, ACC_ATTNO: 61,
     ACC_FFN: 77, ACC_FFN + 1: 85, ACC_LAST: 113})
FULL_COUNT = (15, 16)


def full_count(pair, use):
    return use + 1 - (use > ACC_MIX) - (pair == 0 and use > A_Q)


MISC_FULL = (3, 2)
TP_FULL = (T_USES // 2, T_USES // 2 - 1)


def tp_count(n):
    return n // 2 + 1 - (n % 2 == 1 and n > T_MT + 1)


def hi_count(n):
    return n + 1 if n < T_HC else n - 1 if n < T_P else T_P - 1 if n == T_O0 else n - 9


def p_use(m):
    return T_P + m + (m >= T_O0 - T_P)


def unit_beside(n):
    return U_POOLO + n if n >= 1 else None


def mul_count(n):
    return n + 1 if n < 4 else n - 1 if n < 10 else n - 5 if n < 16 else n - 23


def build(nc, W, par_d, const_d, gain_d, x_d, pos_d, out_d):
    with ExitStack() as ctx:
        def sb(name, shape, dt=F32):
            return ctx.enter_context(nc.sbuf_tensor(name, shape, dt))

        def sem(name):
            return ctx.enter_context(nc.semaphore(name))

        raw = sb("raw", [P, RING, WU])
        w_hi = sb("w_hi", [P, RING, WU], F32R)
        w_lo = sb("w_lo", [P, RING, WU], F32R)
        x = sb("x_sb", [P, TOK, D])
        xT_hi = sb("xT_hi", [P, KD, SEQ], F32R)
        xT_lo = sb("xT_lo", [P, KD, SEQ], F32R)
        hT_hi = sb("hT_hi", [P, FT, SEQ], F32R)
        hT_lo = sb("hT_lo", [P, FT, SEQ], F32R)
        gain = sb("gain", [P, D])
        const = sb("const", [P, NCONST])
        par2 = sb("par2", [P, LAYERS, NPAR])
        par = sb("par", [P, NPAR])
        cq = sb("cq", [P, TOK, Q_RANK + CKV_W])
        hc = sb("hc", [P, TOK, CONV])
        sg = sb("sg", [P, TOK, 512])
        u_sb = sb("u_sb", [P, TOK, 512])
        hcT = sb("hcT", [P, CT, TAPS - 1 + SEQ])
        cacc = sb("cacc", [P, CT, SEQ])
        cacc_odd = sb("cacc_odd", [P, SEQ])
        cprod = sb("cprod", [P, SEQ])
        gates = sb("gates", [P, TOK, 3 * D])
        qk = sb("qk", [P, 2, TOK, HEADS * QK])
        v_sb = sb("v_sb", [P, TOK, HEADS * VDIM])
        tmp = sb("tmp", [P, 2, 512])
        rope_a = sb("rope_a", [P, 256])
        rope_b = sb("rope_b", [P, 256])
        cos2 = sb("cos2", [P, TOK, ROPE])
        sin2 = sb("sin2", [P, TOK, ROPE])
        ang = sb("ang", [P, 6, TOK, HR])
        pos_i = sb("pos_i", [P, TOK], I32)
        pos_f = sb("pos_f", [P, TOK])
        ssq = sb("ssq", [P, NSTAT])
        mean2 = sb("mean2", [P, NSTAT])
        rstd = sb("rstd", [P, NSTAT])
        cvar = sb("cvar", [P, TOK])
        crstd = sb("crstd", [P, TOK])
        half = sb("half", [P, 1])
        mx = sb("mx", [P, 2, 2])
        nmx = sb("nmx", [P, 2, 2])
        rsum = sb("rsum", [P, 2, 2])
        rinv = sb("rinv", [P, 2, 2])

        q_sb, k_sb = qk[:, 0], qk[:, 1]
        qk_flat = qk[:, :, :, :].rearrange("p a t n -> p (a t n)")
        probs = qk_flat[:, 0:1024].rearrange("p (b i n) -> p b i n", b=2, i=2)
        pT = qk_flat[:, 1024:2048].rearrange("p (b i n) -> p b i n", b=2, i=4)
        o_sb = qk_flat[:, 2048:3072].rearrange("p (t n) -> p t n", t=TOK)
        junk = qk_flat[:, 0:D]
        xc = hc[:, :, :].rearrange("p t n -> p (t n)").rearrange("p (c n) -> p c n", c=CT)
        sq = sg[:, :, :].rearrange("p t n -> p (t n)").rearrange("p (c n) -> p c n", c=CT)
        hid = u_sb
        ident = const[:, K_ID:K_ID + P]
        ones = const[:, K_ONE:K_ONE + P]
        mask = const[:, K_MASK:K_MASK + P]

        acc = ctx.enter_context(nc.psum_tensor("acc", [P, 4, 512], F32))
        tp = ctx.enter_context(nc.psum_tensor("tp", [P, 2, 512], F32))
        misc = ctx.enter_context(nc.psum_tensor("misc", [P, 2, 512], F32))

        raw_in = [sem(f"raw_in{s}") for s in range(RING)]
        hi_done = sem("hi_done")
        lo_done = sem("lo_done")
        pool_lo = sem("pool_lo")
        unit_used = sem("unit_used")
        full = [sem(f"full{b}") for b in range(2)]
        wide_full = sem("wide_full")
        free = [sem(f"free{b}") for b in range(4)]
        tp_full = [sem(f"tp_full{b}") for b in range(2)]
        tp_free = [sem(f"tp_free{b}") for b in range(2)]
        tp_hi = sem("tp_hi")
        mul_done = sem("mul_done")
        misc_full = [sem(f"misc_full{b}") for b in range(2)]
        misc_free = [sem(f"misc_free{b}") for b in range(2)]
        d_hi = sem("d_hi")
        const_in = sem("const_in")
        late_in = sem("late_in")
        x_in = [sem(f"x_in{t}") for t in range(TOK)]
        setup = sem("setup")
        ang_ready = sem("ang_ready")
        tables = sem("tables")
        par_ready = sem("par_ready")
        x_ready = [sem(f"x_ready{t}") for t in range(TOK)]
        ssq_done = sem("ssq_done")
        r_done = sem("r_done")
        mean_done = sem("mean_done")
        gain_in = sem("gain_in")
        gain_used = sem("gain_used")
        pad_zero = sem("pad_zero")
        q_roped = sem("q_roped")
        k_roped = sem("k_roped")
        k_nope = sem("k_nope")
        conv_dve = sem("conv_dve")
        pool_step = sem("pool_step")
        pool_went = sem("pool_went")
        conv_pool = sem("conv_pool")
        centred = sem("centred")
        sq_done = sem("sq_done")
        sq_summed = sem("sq_summed")
        var_in = sem("var_in")
        cstd = sem("cstd")
        diag_done = sem("diag_done")
        spread = sem("spread")
        csilu = sem("csilu")
        conv_hi = sem("conv_hi")
        conv_lo = sem("conv_lo")
        s_done = sem("s_done")
        nm_done = sem("nm_done")
        exp_done = sem("exp_done")
        pv_done = sem("pv_done")
        gated = sem("gated")
        summed = sem("summed")
        merged = sem("merged")
        dve_step = sem("dve_step")
        stored = sem("stored")

        block = ctx.enter_context(nc.Block())

        @block.sync
        def _(sp):
            sp.dma_start(x[:, 0, :], x_d[0:P, :]).then_inc(x_in[0], 16)
            sp.dma_start(const[:, 0:K_ONE], const_d[:, 0:K_ONE]).then_inc(const_in, 16)
            sp.dma_start(par2[:, :, :], par_d).then_inc(const_in, 16)
            sp.dma_start(pos_i[:, :], pos_d).then_inc(const_in, 16)

            with sp.Fori(0, LAYERS) as l:
                def load(u, s, width):
                    sp.wait_ge(lo_done, l * UNITS + u + 1)
                    sp.dma_start(raw[:, s, 0:width],
                                 W[bass.ds((l * UNITS + u) * P, P), 0:width]).then_inc(raw_in[s], 16)

                def loads(first, last, width):
                    if last - first < 2 * RING:
                        for u in range(first, last):
                            load(u, u % RING, width)
                        return
                    with sp.Fori(0, (last - first) // RING) as i:
                        for s in range(RING):
                            load(i * RING + (first + s), (first + s) % RING, width)
                    for u in range(first + (last - first) // RING * RING, last):
                        load(u, u % RING, width)

                def load_gain(n):
                    sp.wait_ge(gain_used, l * 4 + 2 * n + 1)
                    sp.dma_start(gain[:, :], gain_d[bass.ds(l * 2 + n, 1), :].to_broadcast((P, D))
                                 ).then_inc(gain_in, 16)

                loads(U_G, U_CQ, 1024)
                load_gain(0)
                loads(U_CQ, U_CKV, 2 * Q_RANK)
                loads(U_CKV, U_Q, 2 * CKV_W)
                loads(U_Q, U_POOL, HEADS * QK)
                loads(U_POOL, U_MT, 1024)
                loads(U_MT, U_GATE, 512)
                loads(U_GATE, U_FFN + 12, 1024)
                load_gain(1)
                loads(U_FFN + 12, UNITS, 1024)

            for t in range(TOK):
                for h in range(2):
                    sp.wait_ge(x_ready[t], 4 * LAYERS + 1 + h)
                    k = slice(512 * h, 512 * (h + 1))
                    sp.dma_start(out_d[t * P:(t + 1) * P, k], x[:, t, k]).then_inc(stored, 16)
            sp.wait_ge(stored, 16 * 2 * TOK)

        @block.tensor
        def _(pe):
            pe.sem_inc(unit_used, RING)
            for b in range(4):
                pe.sem_inc(free[b], 1)
            for b in range(2):
                pe.sem_inc(tp_free[b], 1)
                pe.sem_inc(misc_free[b], 1)
            pe.wait_ge(const_in, 48)

            with pe.Fori(0, LAYERS) as l:
                def mm3(out, a_hi, a_lo, b_hi, b_lo, start, stop):
                    pe.matmul(out, a_hi, b_hi, start=start, stop=False)
                    pe.matmul(out, a_hi, b_lo, start=False, stop=False)
                    return pe.matmul(out, a_lo, b_hi, start=False, stop=stop)

                def unit_ready(u):
                    pe.wait_ge(lo_done, l * UNITS + (RING + u + 1))

                def bank_free(b, use):
                    pe.wait_ge(free[b], l * ACC_USES + (use + 1))

                def tok_mm(u, t, kts, width, banks, srcT, first, last):
                    s_hi, s_lo = srcT
                    s = u % RING
                    for i, kt in enumerate(kts):
                        for g, b in enumerate(banks):
                            c = (i * len(banks) + g) * width
                            mm = mm3(b, s_hi[:, kt, t * P:(t + 1) * P], s_lo[:, kt, t * P:(t + 1) * P],
                                     w_hi[:, s, c:c + width], w_lo[:, s, c:c + width],
                                     kt == first, kt == last)
                    return mm

                XT, HT = (xT_hi, xT_lo), (hT_hi, hT_lo)

                def col_group(u0, n, per, width, pair, use, srcT, kt0=0, before_third=None):
                    for i in range(n):
                        if i == 2 and before_third:
                            before_third()
                        unit_ready(u0 + i)
                        for t in range(TOK):
                            b = 2 * pair + t
                            if i == 0:
                                bank_free(b, use)
                            kts = [kt0 + i * per + k for k in range(per)]
                            mm = tok_mm(u0 + i, t, kts, width, [acc[:, b, 0:width]], srcT,
                                        kt0, kt0 + n * per - 1)
                            if t == 1:
                                mm.then_inc(unit_used, 1)
                            elif i == n - 1:
                                mm.then_inc(full[pair], 1)

                def transposes(n, blocks):
                    b = n % 2
                    pe.wait_ge(tp_free[b], l * (T_USES // 2) + (n // 2 + 1))
                    for i, (src, rows) in enumerate(blocks):
                        mm = pe.transpose(tp[0:rows, b, i * P:(i + 1) * P], src, ident)
                    mm.then_inc(tp_full[b], 1)

                def stored_T(n):
                    pe.wait_ge(tp_free[n % 2], l * (T_USES // 2) + (n // 2 + 2))

                def x_transposes(n0, t, ready):
                    for h in range(2):
                        pe.wait_ge(x_ready[t], l * 4 + (2 * ready - 1 + h))
                        transposes(n0 + 2 * t + h,
                                   [(x[:, t, (4 * h + k) * P:(4 * h + k + 1) * P], P) for k in range(4)])

                def first_group(u0, n0, use, pair, ready, before):
                    for t in range(TOK):
                        stored_T(n0 + 2 * t)
                        stored_T(n0 + 2 * t + 1)
                        bank_free(2 * pair + t, use)
                        for i in range(4):
                            if t == 0:
                                if i == before:
                                    x_transposes(n0, 1, ready)
                                unit_ready(u0 + i)
                            mm = tok_mm(u0 + i, t, [2 * i, 2 * i + 1], 512,
                                        [acc[:, 2 * pair + t, :]], XT, 0, KD - 1)
                            if t == 1:
                                mm.then_inc(unit_used, 1)
                            elif i == 3:
                                mm.then_inc(full[pair], 1)

                def wide_group(u0, n, use, srcT, waits, ahead=None):
                    def one(i, t):
                        if i == 0:
                            bank_free(2 * t, use)
                            bank_free(2 * t + 1, use)
                        mm = tok_mm(u0 + i, t, [i], 512, [acc[:, 2 * t, :], acc[:, 2 * t + 1, :]],
                                    srcT, 0, n - 1)
                        if t == 1:
                            mm.then_inc(unit_used, 1)
                        elif i == n - 1:
                            mm.then_inc(wide_full, 1)

                    for first, last in [(0, 2)] + [(i, i + 1) for i in range(2, n - 4)] + [(n - 4, n)]:
                        for t in range(TOK):
                            for i in range(first, last):
                                if t == 0:
                                    waits(i)
                                    unit_ready(u0 + i)
                                elif i == n - 1 and ahead:
                                    ahead()
                                one(i, t)

                x_transposes(T_X, 0, 1)
                first_group(U_G, T_X, A_G, 0, 1, 1)
                col_group(U_A, 4, 2, 512, 1, B_A, XT)
                col_group(U_CQ, 4, 2, Q_RANK, 0, A_CQ, XT)
                for t in range(TOK):
                    pe.wait_ge(free[2 + t], l * ACC_USES + (B_A + 2))
                    transposes(T_HC + t, [(hc[:, t, c * P:(c + 1) * P], P) for c in range(CT)])
                def cq_transposes():
                    for t in range(TOK):
                        pe.wait_ge(free[t], l * ACC_USES + (A_CQ + 2))
                        transposes(T_CQ + t, [(cq[:, t, c * P:(c + 1) * P], P) for c in range(3)])

                col_group(U_CKV, 4, 2, CKV_W, 1, B_CKV, XT, before_third=cq_transposes)
                for i in range(3):
                    unit_ready(U_Q + i)
                    for t in range(TOK):
                        if i == 0:
                            stored_T(T_CQ + t)
                            bank_free(t, A_Q)
                            pe.wait_ge(misc_free[t], l * (M_USES // 2) + 1)
                        mm = tok_mm(U_Q + i, t, [i], 384, [acc[:, t, 0:384], misc[:, t, 0:384]], HT, 0, 2)
                        if t == 1:
                            mm.then_inc(unit_used, 1)
                        elif i == 2:
                            mm.then_inc(misc_full[0], 1)
                for t in range(TOK):
                    pe.wait_ge(free[2 + t], l * ACC_USES + (B_CKV + 2))
                    transposes(T_CKV + t, [(cq[:, t, c * P:(c + 1) * P], P) for c in range(3, 5)])
                col_group(U_POOL, 4, 2, 512, 1, B_POOL, XT)

                def q_transposes(hh):
                    for t in range(TOK):
                        if hh == 0:
                            pe.wait_ge(q_roped, l * TOK + (t + 1))
                        transposes(T_Q + 2 * hh + t, [(q_sb[:, t, h * QK:(h + 1) * QK], QK)
                                                      for h in range(4 * hh, 4 * hh + 4)])

                q_transposes(0)
                for t in range(TOK):
                    stored_T(T_CKV + t)
                col_group(U_K, 1, 2, 512, 0, A_K, HT, kt0=H_CKV)
                for t in range(TOK):
                    pe.wait_ge(free[2 + t], l * ACC_USES + (B_POOL + 2))
                pe.wait_ge(late_in, 16)
                for h in range(2):
                    pe.wait_ge(misc_free[h], l * (M_USES // 2) + (M_D // 2 + 1))
                    for g in range(2 * h, 2 * h + 2):
                        band = const[:, K_BAND + g * BANDW:K_BAND + (g + 1) * BANDW]
                        c = (g % 2) * SEQ
                        pe.matmul(misc[:, h, c:c + SEQ], u_sb[:, 0, g * P:(g + 1) * P], band[:, 0:SEQ],
                                  start=True, stop=False)
                        mm = pe.matmul(misc[:, h, c + P:c + SEQ], u_sb[:, 1, g * P:(g + 1) * P],
                                       band[:, SEQ:BANDW], start=False, stop=True)
                    mm.then_inc(misc_full[h], 1)
                q_transposes(1)
                col_group(U_V, 1, 2, 512, 1, B_V, HT, kt0=H_CKV)
                unit_ready(U_MT)
                for h in range(2):
                    pe.wait_ge(misc_free[h], l * (M_USES // 2) + (M_D // 2 + 2))
                    b = (T_MT + h) % 2
                    pe.wait_ge(tp_free[b], l * (T_USES // 2) + ((T_MT + h) // 2 + 1))
                    for g in range(2 * h, 2 * h + 2):
                        s = U_MT % RING
                        mm = mm3(tp[:, b, (g % 2) * SEQ:(g % 2 + 1) * SEQ],
                                 w_hi[:, s, g * P:(g + 1) * P], w_lo[:, s, g * P:(g + 1) * P],
                                 hT_hi[:, H_CONV + g, :], hT_lo[:, H_CONV + g, :], True, True)
                    mm.then_inc(tp_full[b] if h == 0 else unit_used, 1)
                with pe.Fori(0, 3) as j:
                    for g in range(2):
                        for i in range(4):
                            u = U_GATE + 4 * g + i
                            pe.wait_ge(lo_done, l * UNITS + j * 8 + (RING + u + 1))
                            for t in range(TOK):
                                b = 2 * g + t
                                if i == 0:
                                    pe.wait_ge(free[b], l * ACC_USES + j + (ACC_GATE + 1))
                                mm = tok_mm(u, t, [2 * i, 2 * i + 1], 512, [acc[:, b, :]], XT, 0, KD - 1)
                                if t == 1:
                                    mm.then_inc(unit_used, 1)
                                elif i == 3:
                                    mm.then_inc(full[g], 1)
                def k_transposes(n):
                    hh, t = n // 2, n % 2
                    if hh == 0:
                        pe.wait_ge(k_roped, l * TOK + (t + 1))
                        pe.wait_ge(k_nope, l * TOK + (t + 1))
                    transposes(T_K + n, [(k_sb[:, t, h * QK:(h + 1) * QK], QK) for h in range(4 * hh, 4 * hh + 4)])

                def out_unit(u, halves=(0, 1)):
                    use = ACC_POOLO + (u - U_POOLO) // 4
                    src = (H_POOL, H_CONV, H_O)[(u - U_POOLO) // 4]
                    i, pair = (u - U_POOLO) % 2, (u - U_POOLO) % 4 // 2
                    if u >= U_ATTNO:
                        i, pair = pair, i
                    for t in halves:
                        if t == 0:
                            unit_ready(u)
                        b = 2 * pair + t
                        if i == 0:
                            bank_free(b, use)
                        mm = tok_mm(u, t, [src + 2 * i, src + 2 * i + 1], 512, [acc[:, b, :]], HT, src, src + 3)
                        if t == 1:
                            mm.then_inc(unit_used, 1)
                        elif i == 1:
                            mm.then_inc(full[pair], 1)

                for n in range(TOK):
                    k_transposes(n)
                for h in range(2):
                    stored_T(T_MT + h)
                out_unit(U_POOLO)
                pe.wait_ge(conv_dve, l * 3 + 3)
                pe.wait_ge(conv_pool, l * CT + CT)
                pe.wait_ge(misc_free[0], l * (M_USES // 2) + (M_MEAN // 2 + 1))
                for c in range(CT):
                    mm = pe.matmul(misc[:, 0, 0:SEQ], ones, cacc[:, c, :], start=c == 0, stop=c == CT - 1)
                mm.then_inc(misc_full[0], 1)
                for n in range(TOK, 4):
                    k_transposes(n)

                def scores(n):
                    hp, t = n // 2, n % 2
                    keys = (t + 1) * P
                    if n == 0 or n == 4:
                        for k in range(2):
                            stored_T(T_K + n // 2 + k)
                    pe.wait_ge(misc_free[n % 2], l * (M_USES // 2) + ((M_S + n) // 2 + 1))
                    for i in range(2):
                        h = 2 * hp + i
                        q = slice(t * P, (t + 1) * P)
                        mm = mm3(misc[:, n % 2, i * keys:(i + 1) * keys],
                                 hT_hi[0:QK, H_Q + h, q], hT_lo[0:QK, H_Q + h, q],
                                 xT_hi[0:QK, h, 0:keys], xT_lo[0:QK, h, 0:keys], True, True)
                    mm.then_inc(s_done, 1)

                def p_transposes(n):
                    t = n % 2
                    pe.wait_ge(exp_done, l * STEPS + (n + 1))
                    transposes(p_use(n), [(probs[:, n % 2, i, k * P:(k + 1) * P], P)
                                          for i in range(2) for k in range(t + 1)])

                def weighted_values(n):
                    hp, t = n // 2, n % 2
                    stored_T(p_use(n))
                    for i in range(2):
                        h = 2 * hp + i
                        for k in range(t + 1):
                            mm = pe.matmul(misc[:, n % 2, i * VDIM:(i + 1) * VDIM],
                                           pT[:, n % 2, i * (t + 1) + k, :],
                                           v_sb[:, k, h * VDIM:(h + 1) * VDIM], start=k == 0, stop=k == t)
                    mm.then_inc(pv_done, 1)

                def o_transposes(n, half):
                    for t in range(TOK):
                        m = 4 * half + 2 + t
                        pe.wait_ge(misc_free[t], l * (M_USES // 2) + ((M_S + m) // 2 + 2))
                    transposes(n, [(o_sb[:, t, c * P:(c + 1) * P], P)
                                   for c in range(2 * half, 2 * half + 2) for t in range(TOK)])

                for n in range(STEPS):
                    u = unit_beside(n)
                    if u == U_CONVO:
                        pe.wait_ge(conv_lo, l + 1)
                    if u and n != 2:
                        out_unit(u, (0,))
                    if n == 1:
                        pe.wait_ge(sq_summed, l + 1)
                        pe.wait_ge(misc_free[1], l * (M_USES // 2) + (M_VAR // 2 + 1))
                        for t in range(TOK):
                            mm = pe.matmul(misc[:, 1, t:t + 1], cacc_odd[:, t * P:(t + 1) * P], ones[:, 0:1],
                                           start=True, stop=True)
                        mm.then_inc(misc_full[1], 1)
                    if n >= 2:
                        weighted_values(n - 2)
                    if u:
                        out_unit(u, (1,))
                    if n == 1:
                        pe.wait_ge(diag_done, l * TOK + TOK)
                        pe.matmul(misc[:, 1, 0:SEQ], ones, rope_a[:, :], start=True, stop=True
                                  ).then_inc(spread, 1)
                        p_transposes(0)
                        out_unit(unit_beside(2), (0,))
                    if n == 5:
                        o_transposes(T_O0, 0)
                    scores(n)
                    if n >= 2:
                        p_transposes(n - 1)
                stored_T(T_O0)
                out_unit(U_ATTNO, (0,))
                weighted_values(STEPS - 2)
                out_unit(U_ATTNO, (1,))
                p_transposes(STEPS - 1)
                out_unit(U_ATTNO + 1, (0,))
                weighted_values(STEPS - 1)
                o_transposes(T_O1, 1)
                out_unit(U_ATTNO + 1, (1,))
                stored_T(T_O1)
                out_unit(U_ATTNO + 2)
                out_unit(U_ATTNO + 3, (0,))

                def merged_transposes(h):
                    for t in range(TOK):
                        pe.wait_ge(merged, l * 4 + (2 * h + t + 1))
                        transposes(T_M + 2 * h + t, [(gates[:, t, (4 * h + k) * P:(4 * h + k + 1) * P], P)
                                                     for k in range(4)])

                merged_transposes(0)
                out_unit(U_ATTNO + 3, (1,))

                def mix_waits(i):
                    if i == 2:
                        merged_transposes(1)
                    if i % 4 == 0:
                        stored_T(T_M + i // 2)
                        stored_T(T_M + i // 2 + 1)

                wide_group(U_MIX, KD, ACC_MIX, XT, mix_waits, lambda: x_transposes(T_F, 0, 2))

                first_group(U_FFN, T_F, ACC_FFN, 0, 2, 2)
                col_group(U_FFN + 4, 4, 2, 512, 1, ACC_FFN, XT)

                with pe.Fori(0, FULL_CHUNKS - 1) as j:
                    for g in range(2):
                        for i in range(4):
                            u = U_FFN + 8 + 4 * g + i
                            pe.wait_ge(lo_done, l * UNITS + j * 8 + (RING + u + 1))
                            for t in range(TOK):
                                b = 2 * g + t
                                if i == 0:
                                    pe.wait_ge(free[b], l * ACC_USES + j + (ACC_FFN + 2))
                                mm = tok_mm(u, t, [2 * i, 2 * i + 1], 512, [acc[:, b, :]], XT, 0, KD - 1)
                                if t == 1:
                                    mm.then_inc(unit_used, 1)
                                elif i == 3:
                                    mm.then_inc(full[g], 1)
                        if g == 0:
                            for t in range(TOK):
                                pe.wait_ge(free[2 + t], l * ACC_USES + j + (ACC_FFN + 2))
                                pe.wait_ge(tp_free[t], l * (T_USES // 2) + j + (T_H // 2 + 1))
                                for c in range(4):
                                    mm = pe.transpose(tp[:, t, c * P:(c + 1) * P],
                                                      hid[:, t, c * P:(c + 1) * P], ident)
                                mm.then_inc(tp_full[t], 1)
                col_group(U_LAST, 2, 4, LAST_W, 0, ACC_LAST, XT)
                for t in range(TOK):
                    pe.wait_ge(free[2 + t], l * ACC_USES + (ACC_LAST + 1))
                    transposes(T_HLAST - 2 + t, [(hid[:, t, c * P:(c + 1) * P], P) for c in range(4)])
                col_group(U_LAST + 2, 2, 4, LAST_W, 1, ACC_LAST, XT)

                def down_waits(i):
                    if i == 2:
                        for t in range(TOK):
                            pe.wait_ge(free[2 + t], l * ACC_USES + (ACC_LAST + 2))
                            transposes(T_HLAST + t, [(hid[:, t, c * P:(c + 1) * P], P) for c in range(2)])
                    if i % 4 == 0:
                        for t in range(TOK):
                            stored_T(T_H + i // 2 + t)

                wide_group(U_DOWN, FT, ACC_DOWN, HT, down_waits)

        @block.scalar
        def _(act):
            act.preload_act_table(ACT.Sigmoid)
            act.wait_ge(raw_in[0], 16)
            act.dma_start(x[:, 1, :], x_d[P:2 * P, :]).then_inc(x_in[1], 16)

            with act.Fori(0, LAYERS) as l:
                def hi(u, off=0, width=None, uses=0):
                    s = u % RING
                    width = width or unit_width(u)
                    act.wait_ge(raw_in[s], l * (16 * UNITS // RING) + uses * 16 + 16 * (u // RING + 1))
                    act.wait_ge(unit_used, l * UNITS + off + (u + 1))
                    act.activation(w_hi[:, s, 0:width], raw[:, s, 0:width], ACT.Copy).then_inc(hi_done, 1)

                def his(first, last):
                    for u in range(first, last):
                        hi(u)

                def bank(b, use, j=None):
                    pair, t = b // 2, b % 2
                    if t == 0:
                        act.wait_ge(full[pair], l * FULL_COUNT[pair] + (0 if j is None else j)
                                   + full_count(pair, use))
                    else:
                        act.wait_ge(unit_used, l * UNITS + (0 if j is None else j * 8)
                                   + (RING + LAST_UNIT[pair][use] + 1))

                def stat(n):
                    act.wait_ge(r_done, l * NSTAT + (n + 1))
                    return rstd[:, n:n + 1]

                def square(n, src, scale=1.0):
                    if n:
                        act.wait_ge(ssq_done, l * NSTAT + n)
                    act.activation(junk[:, 0:src.shape[-1]], src, ACT.Square, scale=scale,
                                   accum_out=ssq[:, n:n + 1]).then_inc(ssq_done, 1)

                def hi_scaled(n, dst):
                    act.wait_ge(mul_done, l * 14 + mul_count(n))
                    w = dst.shape[1] * dst.shape[2]
                    act.activation(dst, tmp[:, n % 2, 0:w].rearrange("p (a b) -> p a b", a=dst.shape[1]),
                                   ACT.Copy).then_inc(tp_hi, 1)

                def hi_T(n, dst, off=0):
                    act.wait_ge(tp_full[n % 2], l * TP_FULL[n % 2] + off + tp_count(n))
                    w = dst.shape[1] * dst.shape[2]
                    act.activation(dst, tp[0:dst.shape[0], n % 2, 0:w].rearrange("p (a b) -> p a b", a=dst.shape[1]),
                                   ACT.Copy).then_inc(tp_hi, 1)

                def tokens(t):
                    return slice(t * P, (t + 1) * P)

                hi(0)
                for h in range(2):
                    hi_scaled(T_X + h, xT_hi[:, 4 * h:4 * h + 4, tokens(0)])
                his(1, 2)
                act.wait_ge(x_ready[0], l * 4 + 2)
                square(R_X, x[:, 0, :])
                his(2, 4)
                for h in range(2):
                    hi_scaled(T_X + 2 + h, xT_hi[:, 4 * h:4 * h + 4, tokens(1)])
                act.wait_ge(x_ready[1], l * 4 + 2)
                square(R_X + 1, x[:, 1, :])
                his(4, 6)
                bank(0, A_G)
                act.activation(sg[:, 0, :], acc[:, 0, :], ACT.Sigmoid, scale=stat(R_X)).then_inc(free[0], 1)
                his(6, 8)
                bank(1, A_G)
                act.activation(sg[:, 1, :], acc[:, 1, :], ACT.Sigmoid, scale=stat(R_X + 1)).then_inc(free[1], 1)
                his(8, 12)
                his(12, 16)
                for t in range(TOK):
                    bank(t, A_CQ)
                    square(R_CQ + t, acc[:, t, 0:Q_RANK], rstd[:, R_X + t:R_X + t + 1])
                    act.activation(cq[:, t, 0:Q_RANK], acc[:, t, 0:Q_RANK], ACT.Copy,
                                   scale=rstd[:, R_X + t:R_X + t + 1]).then_inc(free[t], 1)
                act.wait_ge(pad_zero, 1)
                for t in range(TOK):
                    n = T_HC + t
                    act.wait_ge(tp_full[n % 2], l * TP_FULL[n % 2] + tp_count(n))
                    act.activation(hcT[:, :, TAPS - 1 + t * P:TAPS - 1 + (t + 1) * P],
                                   tp[:, n % 2, :].rearrange("p (c n) -> p c n", c=CT),
                                   ACT.Copy).then_inc(tp_free[n % 2], 1)
                his(16, 18)
                for t in range(TOK):
                    hi_scaled(T_CQ + t, hT_hi[:, H_CQ:H_CQ + 3, tokens(t)])
                his(18, 20)
                for t in range(TOK):
                    bank(2 + t, B_CKV)
                    square(R_CKV + t, acc[:, 2 + t, 0:KV_RANK], rstd[:, R_X + t:R_X + t + 1])
                    act.activation(cq[:, t, Q_RANK:Q_RANK + CKV_W], acc[:, 2 + t, 0:CKV_W], ACT.Copy,
                                   scale=rstd[:, R_X + t:R_X + t + 1]).then_inc(free[2 + t], 1)
                his(20, 23)
                act.wait_ge(ssq_done, l * NSTAT + R_MIX)
                for half in range(2):
                    for t in range(TOK):
                        if t == 0:
                            act.wait_ge(misc_full[0], l * MISC_FULL[0] + 1)
                        else:
                            bank(1, A_Q)
                        src, done = ((acc, free), (misc, misc_free))[half]
                        act.activation(q_sb[:, t, 384 * half:384 * (half + 1)], src[:, t, 0:384], ACT.Copy,
                                       scale=stat(R_CQ + t)).then_inc(done[t], 1)
                for t in range(TOK):
                    hi_scaled(T_CKV + t, hT_hi[:, H_CKV:H_CKV + 2, tokens(t)])
                his(23, 24)
                act.wait_ge(ang_ready, 1)
                act.activation(sin2[:, :, 0:HR], ang[:, 4], ACT.Sin, scale=-1.0)
                act.activation(sin2[:, :, HR:ROPE], ang[:, 4], ACT.Sin)
                act.activation(cos2[:, :, 0:HR], ang[:, 5], ACT.Sin)
                act.activation(cos2[:, :, HR:ROPE], ang[:, 5], ACT.Sin).then_inc(tables, 1)
                his(24, 27)
                for t in range(TOK):
                    bank(2 + t, B_POOL)
                    act.activation(u_sb[:, t, :], acc[:, 2 + t, :], ACT.Copy,
                                   scale=rstd[:, R_X + t:R_X + t + 1]).then_inc(free[2 + t], 1)

                def hi_q(hh):
                    for t in range(TOK):
                        hi_T(T_Q + 2 * hh + t, hT_hi[0:QK, H_Q + 4 * hh:H_Q + 4 * hh + 4, tokens(t)])

                hi_q(0)
                his(27, 28)
                for t in range(TOK):
                    bank(t, A_K)
                    act.activation(k_sb[:, t, :].rearrange("p (h d) -> p h d", h=HEADS)[:, :, 0:NOPE],
                                   acc[:, t, :].rearrange("p (h d) -> p h d", h=HEADS), ACT.Copy,
                                   scale=stat(R_CKV + t)).then_inc(k_nope, 1)
                    act.wait_ge(k_nope, l * TOK + (t + 1))
                    act.sem_inc(free[t], 1)
                for h in range(2):
                    act.wait_ge(misc_full[h], l * MISC_FULL[h] + (2 - h))
                    act.activation(hT_hi[:, H_CONV + 2 * h:H_CONV + 2 * h + 2, :],
                                   misc[:, h, :].rearrange("p (g n) -> p g n", g=2), ACT.Copy).then_inc(d_hi, 1)
                hi_q(1)
                his(28, 29)
                for t in range(TOK):
                    bank(2 + t, B_V)
                    act.activation(v_sb[:, t, :], acc[:, 2 + t, :], ACT.Copy,
                                   scale=rstd[:, R_CKV + t:R_CKV + t + 1]).then_inc(free[2 + t], 1)
                his(29, 30)
                for h in range(2):
                    hi_scaled(T_MT + h, hT_hi[:, H_POOL + 2 * h:H_POOL + 2 * h + 2, :])
                with act.Fori(0, 3) as j:
                    for g in range(2):
                        for i in range(4):
                            hi(U_GATE + 4 + 4 * g + i, j * 8, WU, j * 2)
                        for t in range(TOK):
                            bank(2 * g + t, ACC_GATE, j)
                            act.activation(gates[:, t, bass.ds(j * D + 512 * g, 512)], acc[:, 2 * g + t, :],
                                           ACT.Sigmoid, scale=rstd[:, R_X + t:R_X + t + 1]
                                           ).then_inc(free[2 * g + t], 1)
                for n in range(4):
                    hh, t = n // 2, n % 2
                    if n == 2:
                        his(54, 55)
                    hi_T(T_K + n, xT_hi[0:QK, 4 * hh:4 * hh + 4, tokens(t)])
                act.wait_ge(centred, l + 1)
                act.activation(sq[:, :, :], xc, ACT.Square).then_inc(sq_done, 1)

                def store_p(m):
                    use = p_use(m)
                    act.wait_ge(tp_full[use % 2], l * TP_FULL[use % 2] + tp_count(use))
                    if m >= 2:
                        act.wait_ge(pv_done, l * STEPS + (m - 1))
                    blocks = 2 * (m % 2 + 1)
                    act.activation(pT[:, m % 2, 0:blocks, :],
                                   tp[:, use % 2, 0:blocks * P].rearrange("p (b n) -> p b n", b=blocks),
                                   ACT.Copy).then_inc(tp_free[use % 2], 1)

                def hi_o(n, half):
                    hi_T(n, hT_hi[:, H_O + 2 * half:H_O + 2 * half + 2, :])

                for n in range(STEPS):
                    if n >= 1:
                        hi(unit_beside(n) + RING)
                    if n == 5:
                        hi_o(T_O0, 0)
                    if n >= 1:
                        store_p(n - 1)
                    if n == 1:
                        act.preload_act_table(ACT.Silu)
                        act.wait_ge(par_ready, l + 1)
                        act.wait_ge(misc_free[1], l * (M_USES // 2) + (M_VAR // 2 + 2))
                        for c in range(CT):
                            act.activation(sq[:, c, :], xc[:, c, :], ACT.Silu, scale=par[:, C_LG + c:C_LG + c + 1],
                                           bias=par[:, C_LB + c:C_LB + c + 1]).then_inc(csilu, 1)
                        act.preload_act_table(ACT.Exp)
                    keys = (n % 2 + 1) * P
                    act.wait_ge(nm_done, l * STEPS + (n + 1))
                    for i in range(2):
                        e = act.activation(probs[:, n % 2, i, 0:keys], misc[:, n % 2, i * keys:(i + 1) * keys],
                                           ACT.Exp, scale=SCALE, bias=nmx[:, n % 2, i:i + 1],
                                           accum_out=rsum[:, n % 2, i:i + 1])
                    e.then_inc(exp_done, 1)
                    if n == 1:
                        act.wait_ge(csilu, l * CT + CT)
                        act.activation(hT_hi[:, H_CONV:H_CONV + CT, :], sq[:, :, :], ACT.Copy).then_inc(conv_hi, 1)
                his(62, 63)
                store_p(STEPS - 1)
                hi_o(T_O1, 1)
                his(63, 65)
                for t in range(TOK):
                    hi_T(T_M + t, xT_hi[:, 0:4, tokens(t)])
                his(65, 68)
                for t in range(TOK):
                    hi_T(T_M + 2 + t, xT_hi[:, 4:8, tokens(t)])
                his(68, 70)

                def post_square(n, t, use):
                    if t == 0:
                        act.wait_ge(wide_full, l * 2 + (1 if use == ACC_MIX else 2))
                    else:
                        act.wait_ge(unit_used, l * UNITS + (RING + (U_FFN if use == ACC_MIX else UNITS)))
                    square(n, acc[:, 2 * t:2 * t + 2, :].rearrange("p a n -> p (a n)"))

                post_square(R_MIX, 0, ACC_MIX)
                his(70, 73)
                for h in range(2):
                    hi_scaled(T_F + h, xT_hi[:, 4 * h:4 * h + 4, tokens(0)])
                post_square(R_MIX + 1, 1, ACC_MIX)
                his(73, 74)
                act.wait_ge(x_ready[0], l * 4 + 4)
                square(R_F, x[:, 0, :])
                for h in range(2):
                    hi_scaled(T_F + 2 + h, xT_hi[:, 4 * h:4 * h + 4, tokens(1)])
                act.wait_ge(x_ready[1], l * 4 + 4)
                square(R_F + 1, x[:, 1, :])
                his(74, 78)
                for t in range(TOK):
                    bank(t, ACC_FFN)
                    act.activation(sg[:, t, :], acc[:, t, :], ACT.Silu, scale=stat(R_F + t)
                                   ).then_inc(free[t], 1)
                his(78, 82)
                with act.Fori(0, FULL_CHUNKS - 1) as j:
                    for i in range(4):
                        hi(U_FFN + 12 + i, j * 8, WU, j * 2)
                    for t in range(TOK):
                        bank(t, ACC_FFN + 1, j)
                        act.wait_ge(free[2 + t], l * ACC_USES + j + (ACC_FFN + 2))
                        act.activation(sg[:, t, :], acc[:, t, :], ACT.Silu,
                                       scale=rstd[:, R_F + t:R_F + t + 1]).then_inc(free[t], 1)
                    for t in range(TOK):
                        act.wait_ge(tp_full[t], l * TP_FULL[t] + j + tp_count(T_H + t))
                        act.activation(hT_hi[:, bass.ds(j * 4, 4), tokens(t)],
                                       tp[:, t, :].rearrange("p (a b) -> p a b", a=4), ACT.Copy).then_inc(tp_hi, 1)
                    for i in range(4):
                        hi(U_FFN + 16 + i, j * 8, WU, j * 2)
                his(114, 116)
                for t in range(TOK):
                    bank(t, ACC_LAST)
                    act.wait_ge(free[2 + t], l * ACC_USES + (ACC_LAST + 1))
                    act.activation(sg[:, t, 0:LAST_W], acc[:, t, 0:LAST_W], ACT.Silu,
                                   scale=rstd[:, R_F + t:R_F + t + 1]).then_inc(free[t], 1)
                for t in range(TOK):
                    hi_T(T_HLAST - 2 + t, hT_hi[:, FT - 6:FT - 2, tokens(t)])
                his(116, 120)
                for t in range(TOK):
                    hi_T(T_HLAST + t, hT_hi[:, FT - 2:FT, tokens(t)])
                his(120, 136)
                act.preload_act_table(ACT.Sigmoid)
                for t in range(TOK):
                    post_square(R_DOWN + t, t, ACC_DOWN)

        @block.vector
        def _(dve):
            def f(ap):
                return ap.bitcast(F32)

            dve.sem_inc(lo_done, RING)
            dve.sem_inc(gain_used, 1)
            dve.memset(hcT[:, :, 0:TAPS - 1], 0.0).then_inc(pad_zero, 1)

            dve.wait_ge(const_in, 48)

            with dve.Fori(0, LAYERS) as l:
                steps = [0]

                def step(ins):
                    steps[0] += 1
                    ins.then_inc(dve_step, 1)
                    dve.wait_ge(dve_step, l * DVE_STEPS + steps[0])

                def lo(u, off=0, width=None):
                    if u in POOL_UNITS:
                        dve.wait_ge(pool_lo, l * len(POOL_UNITS) + POOL_UNITS.index(u) + 1)
                        dve.sem_inc(lo_done, 1)
                        return
                    s = u % RING
                    width = width or unit_width(u)
                    dve.wait_ge(hi_done, l * UNITS + off + (u + 1))
                    dve.tensor_tensor(w_lo[:, s, 0:width], raw[:, s, 0:width], f(w_hi[:, s, 0:width]),
                                      ALU.subtract).then_inc(lo_done, 1)

                def los(first, last):
                    for u in range(first, last):
                        lo(u)

                def tokens(t):
                    return slice(t * P, (t + 1) * P)

                def split3(ap, a):
                    return ap.rearrange("p (a b) -> p a b", a=a)

                def scaled(n, tiles, width, col):
                    if n == T_MT + 1:
                        dve.wait_ge(unit_used, l * UNITS + (RING + U_MT + 1))
                    else:
                        dve.wait_ge(tp_full[n % 2], l * TP_FULL[n % 2] + tp_count(n))
                    g = par[:, col:col + tiles].unsqueeze(2).to_broadcast((P, tiles, width))
                    dve.tensor_tensor(split3(tmp[:, n % 2, 0:tiles * width], tiles),
                                      split3(tp[:, n % 2, 0:tiles * width], tiles), g, ALU.mult
                                      ).then_inc(mul_done, 1)

                def lo_scaled(n, dst, src_hi):
                    dve.wait_ge(tp_hi, l * 40 + hi_count(n))
                    a = dst.shape[1]
                    dve.tensor_tensor(dst, split3(tmp[:, n % 2, 0:a * dst.shape[2]], a), f(src_hi),
                                      ALU.subtract).then_inc(tp_free[n % 2], 1)

                def lo_T(n, dst, src_hi):
                    dve.wait_ge(tp_hi, l * 40 + hi_count(n))
                    a = dst.shape[1]
                    dve.tensor_tensor(dst, split3(tp[0:dst.shape[0], n % 2, 0:a * dst.shape[2]], a), f(src_hi),
                                      ALU.subtract).then_inc(tp_free[n % 2], 1)

                def x_parts(n0, t, col, between=None):
                    for h in range(2):
                        scaled(n0 + 2 * t + h, 4, P, col + 4 * h)
                    if between is not None:
                        lo(between)
                    for h in range(2):
                        k = slice(4 * h, 4 * h + 4)
                        lo_scaled(n0 + 2 * t + h, xT_lo[:, k, tokens(t)], xT_hi[:, k, tokens(t)])

                def bank(b, use, j=None):
                    pair, t = b // 2, b % 2
                    if t == 0:
                        dve.wait_ge(full[pair], l * FULL_COUNT[pair] + (0 if j is None else j)
                                   + full_count(pair, use))
                    else:
                        dve.wait_ge(unit_used, l * UNITS + (0 if j is None else j * 8)
                                   + (RING + LAST_UNIT[pair][use] + 1))

                def rope(dst, src, t, heads):
                    n = src.shape[1]
                    c = cos2[:, t, :].unsqueeze(1).to_broadcast((P, n, ROPE))
                    s0 = sin2[:, t, 0:HR].unsqueeze(1).to_broadcast((P, n, HR))
                    s1 = sin2[:, t, HR:ROPE].unsqueeze(1).to_broadcast((P, n, HR))
                    a, b = split3(rope_a[:, 0:n * ROPE], n), split3(rope_b[:, 0:n * ROPE], n)
                    dve.tensor_tensor(a, src, c, ALU.mult)
                    dve.tensor_tensor(b[:, :, 0:HR], src[:, :, HR:ROPE], s0, ALU.mult)
                    step(dve.tensor_tensor(b[:, :, HR:ROPE], src[:, :, 0:HR], s1, ALU.mult))
                    if n < heads:
                        a, b = a.to_broadcast((P, heads, ROPE)), b.to_broadcast((P, heads, ROPE))
                    return dve.tensor_tensor(dst, a, b, ALU.add)

                step(dve.tensor_copy(par[:, :], par2[:, bass.ds(l, 1), :].rearrange("p a n -> p (a n)")))
                dve.sem_inc(par_ready, 1)
                x_parts(T_X, 0, C_PRE, between=0)
                los(1, 3)
                x_parts(T_X, 1, C_PRE)
                los(3, 12)
                for t in range(TOK):
                    bank(2 + t, B_A)
                    dve.wait_ge(free[t], l * ACC_USES + (A_G + 2))
                    dve.wait_ge(r_done, l * NSTAT + (R_X + t + 1))
                    dve.scalar_tensor_tensor(out=hc[:, t, :], in0=acc[:, 2 + t, :], scalar=rstd[:, R_X + t:R_X + t + 1],
                                             in1=sg[:, t, :], op0=ALU.mult, op1=ALU.mult).then_inc(free[2 + t], 1)
                los(12, 18)
                for t in range(TOK):
                    scaled(T_CQ + t, 3, P, C_QN)
                for t in range(TOK):
                    lo_scaled(T_CQ + t, hT_lo[:, H_CQ:H_CQ + 3, tokens(t)], hT_hi[:, H_CQ:H_CQ + 3, tokens(t)])
                los(18, 23)
                for t in range(TOK):
                    scaled(T_CKV + t, 2, P, C_KVN)
                for t in range(TOK):
                    lo_scaled(T_CKV + t, hT_lo[:, H_CKV:H_CKV + 2, tokens(t)], hT_hi[:, H_CKV:H_CKV + 2, tokens(t)])
                los(23, 25)
                dve.wait_ge(tables, l + 1)
                for t in range(TOK):
                    dve.wait_ge(free[t], l * ACC_USES + (A_Q + 2))
                    dve.wait_ge(misc_free[t], l * (M_USES // 2) + 2)
                    if t == 1:
                        dve.wait_ge(q_roped, l * TOK + 1)
                    qr = split3(q_sb[:, t, :], HEADS)[:, :, NOPE:QK]
                    rope(qr, qr, t, HEADS).then_inc(q_roped, 1)
                los(25, 26)
                for t in range(TOK):
                    dve.wait_ge(free[2 + t], l * ACC_USES + (B_CKV + 2))
                    k0 = Q_RANK + KV_RANK
                    if t == 0:
                        dve.wait_ge(q_roped, l * TOK + 2)
                    else:
                        dve.wait_ge(k_roped, l * TOK + 1)
                    rope(split3(k_sb[:, t, :], HEADS)[:, :, NOPE:QK], cq[:, t, k0:k0 + ROPE].unsqueeze(1), t, HEADS
                         ).then_inc(k_roped, 1)
                los(26, 27)

                def lo_q(hh):
                    for t in range(TOK):
                        k = slice(H_Q + 4 * hh, H_Q + 4 * hh + 4)
                        lo_T(T_Q + 2 * hh + t, hT_lo[0:QK, k, tokens(t)], hT_hi[0:QK, k, tokens(t)])

                lo_q(0)
                los(27, 28)
                for h in range(2):
                    dve.wait_ge(d_hi, l * 2 + (h + 1))
                    k = slice(H_CONV + 2 * h, H_CONV + 2 * h + 2)
                    dve.tensor_tensor(hT_lo[:, k, :], split3(misc[:, h, :], 2), f(hT_hi[:, k, :]),
                                      ALU.subtract).then_inc(misc_free[h], 1)
                lo_q(1)
                los(28, 30)
                for h in range(2):
                    scaled(T_MT + h, 2, SEQ, C_PS + 2 * h)
                for h in range(2):
                    k = slice(H_POOL + 2 * h, H_POOL + 2 * h + 2)
                    lo_scaled(T_MT + h, hT_lo[:, k, :], hT_hi[:, k, :])

                done0 = steps[0]
                with dve.Fori(0, 3) as j:
                    def tap(k, even, odd):
                        src = hcT[:, bass.ds(j, 1), k:k + SEQ].rearrange("p a n -> p (a n)")
                        w = par[:, bass.ds(j * TAPS + (C_CW + k), 1)]
                        if k == 0:
                            dve.wait_ge(conv_pool, l * CT + j + 1)
                        if k >= 2:
                            dve.wait_ge(dve_step, l * DVE_STEPS + j * (OWN + 1) + (done0 + k - 1))
                        if k == 1:
                            ins = dve.tensor_scalar(odd, src, w, None, ALU.mult)
                        else:
                            s = even if k % 2 == 0 else odd
                            ins = dve.scalar_tensor_tensor(out=s, in0=src, scalar=w, in1=s, op0=ALU.mult, op1=ALU.add)
                        ins.then_inc(dve_step, 1)

                    even = cacc[:, bass.ds(j, 1), :].rearrange("p a n -> p (a n)")
                    odd = cacc_odd[:, :]
                    for i in range(8):
                        if i == 7:
                            dve.wait_ge(dve_step, l * DVE_STEPS + j * (OWN + 1) + (done0 + OWN))
                            dve.tensor_tensor(even, even, odd, ALU.add).then_inc(conv_dve, 1)
                        lo(U_GATE + 4 + i, j * 8, WU)
                        for k in range((OWN * i + 6) // 7, min((OWN * (i + 1) + 6) // 7, OWN)):
                            tap(k, even, odd)
                    dve.wait_ge(conv_dve, l * 3 + j + 1)
                    dve.sem_inc(dve_step, 1)
                steps[0] += 3 * (OWN + 1)

                def lo_k(hh):
                    for t in range(TOK):
                        k = slice(4 * hh, 4 * hh + 4)
                        lo_T(T_K + 2 * hh + t, xT_lo[0:QK, k, tokens(t)], xT_hi[0:QK, k, tokens(t)])

                lo_k(0)
                dve.wait_ge(misc_full[0], l * MISC_FULL[0] + 3)
                dve.tensor_tensor(xc, cacc[:, :, :], misc[:, 0:1, 0:SEQ].to_broadcast((P, CT, SEQ)),
                                  ALU.subtract).then_inc(misc_free[0], 1)
                dve.wait_ge(misc_free[0], l * (M_USES // 2) + (M_MEAN // 2 + 2))
                dve.sem_inc(centred, 1)
                los(54, 55)

                def gate(branch, h, t, use):
                    b = 2 * h + t
                    bank(b, use)
                    g = gates[:, t, branch * D + 512 * h:branch * D + 512 * (h + 1)]
                    return dve.tensor_tensor(g, g, acc[:, b, :], ALU.mult)

                def divide(m):
                    hp, t = m // 2, m % 2
                    dve.wait_ge(pv_done, l * STEPS + (m + 1))
                    step(dve.reciprocal(rinv[:, m % 2, :], rsum[:, m % 2, :]))
                    dve.tensor_tensor(split3(o_sb[:, t, 2 * hp * VDIM:2 * (hp + 1) * VDIM], 2),
                                      split3(misc[:, m % 2, 0:2 * VDIM], 2),
                                      rinv[:, m % 2, :].unsqueeze(2).to_broadcast((P, 2, VDIM)),
                                      ALU.mult).then_inc(misc_free[m % 2], 1)

                def gate_beside(n):
                    branch, h, t = (2, 2, 1)[(n - 2) // 2], (0, 1, 0)[(n - 2) // 2], n % 2
                    gate(branch, h, t, ACC_POOLO if branch == 2 else ACC_CONVO).then_inc(free[2 * h + t], 1)

                def lo_o(n, half):
                    k = slice(H_O + 2 * half, H_O + 2 * half + 2)
                    lo_T(n, hT_lo[:, k, :], hT_hi[:, k, :])

                dve.wait_ge(sq_done, l + 1)
                dve.tensor_reduce(cacc_odd[:, :], sq.rearrange("p c n -> p n c"), AX_X, ALU.add
                                  ).then_inc(sq_summed, 1)
                for n in range(STEPS):
                    if n == 1:
                        dve.wait_ge(spread, l + 1)
                        dve.tensor_tensor(xc, xc, misc[:, 1:2, 0:SEQ].to_broadcast((P, CT, SEQ)),
                                          ALU.mult).then_inc(misc_free[1], 1)
                    if n in (3, 5, 7):
                        gate_beside(n)
                    if n >= 2:
                        divide(n - 2)
                    t = n % 2
                    keys = (t + 1) * P
                    s = split3(misc[:, n % 2, 0:2 * keys], 2)
                    dve.wait_ge(s_done, l * STEPS + (n + 1))
                    step(dve.tensor_tensor(s[:, :, t * P:keys], s[:, :, t * P:keys],
                                           mask.unsqueeze(1).to_broadcast((P, 2, P)), ALU.add))
                    step(dve.tensor_reduce(mx[:, n % 2, :], s, AX_X, ALU.max))
                    dve.tensor_scalar(nmx[:, n % 2, :], mx[:, n % 2, :], -SCALE, None, ALU.mult
                                      ).then_inc(nm_done, 1)
                    if n == 0:
                        dve.wait_ge(misc_full[1], l * MISC_FULL[1] + 2)
                        dve.tensor_scalar(cvar[:, :], misc[:, 1, 0:TOK], EPS, None, ALU.add).then_inc(var_in, 1)
                        lo_k(1)
                        dve.wait_ge(cstd, l + 1)
                        for t in range(TOK):
                            dve.tensor_scalar(rope_a[:, tokens(t)], ident, crstd[:, t:t + 1], float(CONV),
                                              ALU.mult, ALU.mult).then_inc(diag_done, 1)
                    if n in (1, 2, 4, 6):
                        lo(unit_beside(n) + RING)
                    if n in (2, 4, 6):
                        gate_beside(n)
                    if n in (3, 5, 7):
                        lo(unit_beside(n) + RING)
                    if n == 2:
                        dve.wait_ge(conv_hi, l + 1)
                        dve.tensor_tensor(hT_lo[:, H_CONV:H_CONV + CT, :], sq[:, :, :],
                                          f(hT_hi[:, H_CONV:H_CONV + CT, :]), ALU.subtract).then_inc(conv_lo, 1)
                    if n == 5:
                        lo_o(T_O0, 0)
                gate(1, 1, 0, ACC_CONVO).then_inc(free[2], 1)
                divide(STEPS - 2)
                gate(1, 1, 1, ACC_CONVO).then_inc(free[3], 1)
                divide(STEPS - 1)
                los(62, 63)
                lo_o(T_O1, 1)

                def merge(h):
                    for t in range(TOK):
                        gate(0, h, t, ACC_ATTNO).then_inc(free[2 * h + t], 1)
                        dve.wait_ge(free[2 * h + t], l * ACC_USES + (ACC_ATTNO + 2))
                        dve.wait_ge(summed, l * 4 + (2 * h + t + 1))
                        g = gates[:, t, 512 * h:512 * (h + 1)]
                        dve.tensor_tensor(g, g, gates[:, t, 2 * D + 512 * h:2 * D + 512 * (h + 1)],
                                          ALU.add).then_inc(merged, 1)

                los(63, 64)
                merge(0)
                los(64, 65)
                for t in range(TOK):
                    lo_T(T_M + t, xT_lo[:, 0:4, tokens(t)], xT_hi[:, 0:4, tokens(t)])
                merge(1)
                los(65, 68)
                for t in range(TOK):
                    lo_T(T_M + 2 + t, xT_lo[:, 4:8, tokens(t)], xT_hi[:, 4:8, tokens(t)])
                los(68, 70)

                def post_norm(n, t, use, which):
                    dve.wait_ge(r_done, l * NSTAT + (n + 1))
                    dve.wait_ge(gain_in, l * 32 + 16 * (which + 1))
                    y = gates[:, t, D:2 * D]
                    for h in range(2):
                        dve.scalar_tensor_tensor(out=y[:, 512 * h:512 * (h + 1)], in0=acc[:, 2 * t + h, :],
                                                 scalar=rstd[:, n:n + 1], in1=gain[:, 512 * h:512 * (h + 1)],
                                                 op0=ALU.mult, op1=ALU.mult).then_inc(free[2 * t + h], 1)
                    for h in range(2):
                        dve.wait_ge(free[2 * t + h], l * ACC_USES + (use + 2))
                        if h == 1:
                            dve.sem_inc(gain_used, 1)
                        k = slice(512 * h, 512 * (h + 1))
                        dve.tensor_tensor(x[:, t, k], x[:, t, k], y[:, k], ALU.add).then_inc(x_ready[t], 1)

                post_norm(R_MIX, 0, ACC_MIX, 0)
                los(70, 71)
                x_parts(T_F, 0, C_PREF)
                los(71, 73)
                post_norm(R_MIX + 1, 1, ACC_MIX, 0)
                x_parts(T_F, 1, C_PREF)
                los(73, 82)

                def hidden(t, use, width, j=None):
                    bank(2 + t, use, j)
                    dve.wait_ge(free[t], l * ACC_USES + (0 if j is None else j) + (use + 2))
                    n = R_F + t
                    dve.wait_ge(r_done, l * NSTAT + (n + 1))
                    dve.scalar_tensor_tensor(out=hid[:, t, 0:width], in0=acc[:, 2 + t, 0:width],
                                             scalar=rstd[:, n:n + 1], in1=sg[:, t, 0:width],
                                             op0=ALU.mult, op1=ALU.mult).then_inc(free[2 + t], 1)

                for t in range(TOK):
                    hidden(t, ACC_FFN, 512)
                with dve.Fori(0, FULL_CHUNKS - 1) as j:
                    for i in range(4):
                        lo(U_FFN + 12 + i, j * 8, WU)
                    for t in range(TOK):
                        dve.wait_ge(tp_hi, l * 40 + j * 2 + (hi_count(T_H) + t))
                        dve.tensor_tensor(hT_lo[:, bass.ds(j * 4, 4), tokens(t)], split3(tp[:, t, :], 4),
                                          f(hT_hi[:, bass.ds(j * 4, 4), tokens(t)]), ALU.subtract
                                          ).then_inc(tp_free[t], 1)
                    for i in range(4):
                        lo(U_FFN + 16 + i, j * 8, WU)
                    for t in range(TOK):
                        hidden(t, ACC_FFN + 1, 512, j)
                los(114, 116)
                for t in range(TOK):
                    lo_T(T_HLAST - 2 + t, hT_lo[:, FT - 6:FT - 2, tokens(t)], hT_hi[:, FT - 6:FT - 2, tokens(t)])
                los(116, 118)
                for t in range(TOK):
                    hidden(t, ACC_LAST, LAST_W)
                los(118, 120)
                for t in range(TOK):
                    lo_T(T_HLAST + t, hT_lo[:, FT - 2:FT, tokens(t)], hT_hi[:, FT - 2:FT, tokens(t)])
                los(120, 136)
                for t in range(TOK):
                    post_norm(R_DOWN + t, t, ACC_DOWN, 1)
                assert steps[0] == DVE_STEPS, steps[0]

        @block.gpsimd
        def _(pool):
            count = [0]
            pool.memset(half[:, :], -0.5).then_inc(pool_step, 1)
            pool.wait_ge(pool_step, 1)
            for t in range(TOK):
                pool.wait_ge(x_in[t], 16)
                pool.sem_inc(x_ready[t], 2)
            pool.wait_ge(const_in, 48)

            linked = [0]

            def link(ins):
                linked[0] += 1
                ins.then_inc(setup, 1)
                pool.wait_ge(setup, linked[0])

            link(pool.tensor_copy(pos_f[:, :], pos_i[:, :]))
            freq = const[:, K_FREQ:K_FREQ + HR]
            for t in range(TOK):
                link(pool.tensor_scalar(ang[:, 0, t, :], freq, pos_f[:, t:t + 1], None, ALU.mult))
            for which, shift in ((4, 0.0), (5, 0.25)):
                turns, back, part = ang[:, 1], ang[:, 2], ang[:, 3]
                link(pool.tensor_scalar(turns, ang[:, 0], 1.0 / TWO_PI, shift, ALU.mult, ALU.add))
                link(pool.tensor_scalar(turns, turns, ROUND, None, ALU.add))
                link(pool.tensor_scalar(turns, turns, ROUND, None, ALU.subtract))
                src = ang[:, 0]
                for c in TURN:
                    link(pool.tensor_scalar(part, turns, c, None, ALU.mult))
                    link(pool.tensor_tensor(back, src, part, ALU.subtract))
                    src = back
                link(pool.tensor_scalar(back, back, shift * TWO_PI, PI_BELOW, ALU.add, ALU.min))
                link(pool.tensor_scalar(ang[:, which], back, -PI_BELOW, None, ALU.max))
            pool.sem_inc(ang_ready, 1)
            pool.dma_start(const[:, K_ONE:NCONST], const_d[:, K_ONE:NCONST]).then_inc(late_in, 16)
            POOL_STEPS = (CT - 1) * (2 * SHARE - 1) + 2 * TAPS - 1

            with pool.Fori(0, LAYERS) as l:
                def before_scalar():
                    pool.sem_inc(pool_went, 1)

                def norm(n):
                    pool.wait_ge(ssq_done, l * NSTAT + (n + 1))
                    before_scalar()
                    pool.tensor_scalar(mean2[:, n:n + 1], ssq[:, n:n + 1], 1.0 / STAT_WIDTH[n], EPS,
                                       ALU.mult, ALU.add).then_inc(mean_done, 1)
                    pool.wait_ge(mean_done, l * NSTAT + (n + 1))
                    pool.tensor_tensor(rstd[:, n:n + 1], mean2[:, n:n + 1], half[:, :], ALU.pow
                                       ).then_inc(r_done, 1)

                def lo(u):
                    s = u % RING
                    pool.wait_ge(hi_done, l * UNITS + (u + 1))
                    pool.tensor_tensor(w_lo[:, s, :], raw[:, s, :], w_hi[:, s, :].bitcast(F32), ALU.subtract
                                       ).then_inc(pool_lo, 1)

                for n in range(R_CKV):
                    norm(n)
                for t in range(TOK):
                    pool.wait_ge(tp_free[(T_HC + t) % 2], l * (T_USES // 2) + ((T_HC + t) // 2 + 2))
                pool.wait_ge(par_ready, l + 1)
                before_scalar()
                done = 1

                def chained(ins, done):
                    ins.then_inc(pool_step, 1)
                    pool.wait_ge(pool_step, l * POOL_STEPS + done)

                for c in range(CT):
                    first = OWN if c < CT - 1 else 0
                    for k in range(first, TAPS):
                        src = hcT[:, c, k:k + SEQ]
                        w = par[:, C_CW + c * TAPS + k:C_CW + c * TAPS + k + 1]
                        if k == first:
                            done += 1
                            chained(pool.tensor_scalar(cacc[:, c, :], src, w, par[:, C_CB + c:C_CB + c + 1],
                                                       ALU.mult, ALU.add), done)
                        else:
                            done += 2
                            chained(pool.tensor_scalar(cprod[:, :], src, w, None, ALU.mult), done - 1)
                            chained(pool.tensor_tensor(cacc[:, c, :], cacc[:, c, :], cprod[:, :], ALU.add), done)
                        before_scalar()
                    pool.sem_inc(conv_pool, 1)
                    if c == 0:
                        norm(R_CKV)
                        norm(R_CKV + 1)
                assert done == POOL_STEPS + 1
                pool.wait_ge(var_in, l + 1)
                pool.tensor_tensor(crstd[:, :], cvar[:, :], half[:, :].to_broadcast((P, TOK)), ALU.pow
                                   ).then_inc(cstd, 1)
                for h in range(2):
                    for t in range(TOK):
                        b = 2 * h + t
                        pool.wait_ge(free[b], l * ACC_USES + (ACC_CONVO + 2))
                        s = gates[:, t, 2 * D + 512 * h:2 * D + 512 * (h + 1)]
                        pool.tensor_tensor(s, s, gates[:, t, D + 512 * h:D + 512 * (h + 1)], ALU.add
                                           ).then_inc(summed, 1)
                norm(R_MIX)
                lo(70)
                lo(71)
                norm(R_MIX + 1)
                lo(73)
                for n in range(R_F, NSTAT):
                    norm(n)


def unit_width(u):
    if U_CQ <= u < U_CKV:
        return 2 * Q_RANK
    if U_CKV <= u < U_Q:
        return 2 * CKV_W
    if U_Q <= u < U_POOL:
        return HEADS * QK
    return 512 if u == U_MT else WU


def weight_stream(a):
    out = np.zeros((LAYERS, UNITS, P, WU), np.float32)

    def put(u0, w, per):
        L, K, n = w.shape
        t = w.reshape(L, K // (P * per), per, P, n).transpose(0, 1, 3, 2, 4)
        out[:, u0:u0 + K // (P * per), :, 0:per * n] = t.reshape(L, K // (P * per), P, per * n)

    w = a["w_in"]
    edges = np.cumsum([0, Q_RANK, KV_RANK + ROPE, CONV, CONV, 512, 3 * D])
    c_q, c_kv, conv_a, conv_g, pool, gate = (w[:, :, edges[i]:edges[i + 1]] for i in range(6))
    put(U_G, conv_g, 2)
    put(U_A, conv_a, 2)
    put(U_CQ, c_q, 2)
    put(U_CKV, c_kv, 2)
    put(U_POOL, pool, 2)
    put(U_Q, a["w_uq"], 1)
    put(U_K, a["w_uk"], 2)
    put(U_V, a["w_uv"], 2)
    pw = a["pool_w"]
    put(U_MT, pw.transpose(0, 2, 1, 3).reshape(LAYERS, P, 4 * P), 1)
    for g in range(6):
        put(U_GATE + 4 * g, gate[:, :, 512 * g:512 * (g + 1)], 2)
    for g in range(2):
        n = slice(512 * g, 512 * (g + 1))
        put(U_POOLO + 2 * g, a["w_pool_o"][:, :, n], 2)
        put(U_CONVO + 2 * g, a["w_conv_o"][:, :, n], 2)
        for half in range(2):
            put(U_ATTNO + 2 * half + g, a["w_attn_o"][:, 2 * P * half:2 * P * (half + 1), n], 2)
    put(U_MIX, a["w_mix_o"], 1)
    for g in range(FULL_CHUNKS):
        for i, name in enumerate(("w_gate", "w_up")):
            put(U_FFN + 8 * g + 4 * i, a[name][:, :, 512 * g:512 * (g + 1)], 2)
    for i, name in enumerate(("w_gate", "w_up")):
        put(U_LAST + 2 * i, a[name][:, :, 512 * FULL_CHUNKS:], 4)
    put(U_DOWN, a["w_down"], 1)
    return out.reshape(LAYERS * UNITS * P, WU)


def parameters(a):
    cols = [a[name].reshape(LAYERS, -1, P).transpose(2, 0, 1)
            for name in ("mix_norm_pre", "ffn_norm_pre", "q_norm", "kv_norm", "pool_scale",
                         "conv_b", "conv_ln_g", "conv_ln_b")]
    cw = a["conv_w"].reshape(LAYERS, TAPS, CT, P).transpose(3, 0, 2, 1).reshape(P, LAYERS, CT * TAPS)
    return np.ascontiguousarray(np.concatenate(cols + [cw], axis=2))


def constants():
    c = np.zeros((P, NCONST), np.float32)
    c[:, K_ID:K_ID + P] = np.eye(P)
    c[:, K_ONE:K_ONE + P] = 1.0 / CONV
    c[:, K_MASK:K_MASK + P] = np.triu(np.full((P, P), MASKED, np.float32), 1)
    s, t = np.arange(SEQ)[:, None], np.arange(SEQ)[None, :]
    for g, w in enumerate(POOL_WINDOWS):
        band = np.where((s <= t) & (s > t - w), 1.0 / np.minimum(t + 1, w), 0.0) - (s == t)
        c[:, K_BAND + g * BANDW:K_BAND + g * BANDW + SEQ] = band[0:P]
        c[:, K_BAND + g * BANDW + SEQ:K_BAND + (g + 1) * BANDW] = band[P:, P:]
    c[:, K_FREQ:K_FREQ + HR] = np.power(np.float32(10000.0),
                                        -np.arange(0, ROPE, 2, dtype=np.float32) / np.float32(ROPE))
    return c


def kernel(**inputs):
    import concourse.bacc as bacc
    from concourse.bass_utils import run_bass_kernel_spmd

    a = {k: np.asarray(v) for k, v in inputs.items()}
    arrays = {
        "weights": weight_stream(a),
        "params": parameters(a),
        "consts": constants(),
        "gains": np.ascontiguousarray(np.stack([a["mix_norm_post"], a["ffn_norm_post"]], 1).reshape(2 * LAYERS, D)),
        "x_rows": np.ascontiguousarray(a["x"].reshape(SEQ, D)),
        "pos": np.ascontiguousarray(a["positions"].reshape(TOK, P).T),
    }
    nc = bacc.Bacc("TRN2", target_bir_lowering=False, num_devices=1)
    args = [nc.dram_tensor(name, v.shape, mybir.dt.from_np(v.dtype), kind="ExternalInput").ap()
            for name, v in arrays.items()]
    out = nc.dram_tensor("out_rows", (SEQ, D), F32, kind="ExternalOutput").ap()
    build(nc, *args, out)
    r = run_bass_kernel_spmd(nc, [arrays], core_ids=[0])
    return r.results[0]["out_rows"].reshape(1, SEQ, D)
```
